# Optimizing a Trainium2 kernel written in Bass

```python
import jax, jax.numpy as jnp
from jax import lax
import numpy as np

D_MODEL = 1024
BATCH = 1
SEQ = 256
DEPTH = 2

HEAD_DIM = 64
N_HEADS_SB = 8
N_HEADS_RET = 8
N_HEADS_SWA = 16
N_KV_SWA = 4
WINDOW = 128
Q_BLOCK = 128
RET_CHUNK = 128
ROPE_THETA = 10000.0
N_GROUPS = 4
EXPERTS_PER_GROUP = 8
N_EXPERTS = N_GROUPS * EXPERTS_PER_GROUP
TOP_K_IN_GROUP = 2
D_EXPERT = 512
MOE_BLOCK = 256
EPS = 1e-6

W_SB = N_HEADS_SB * HEAD_DIM
W_RET = N_HEADS_RET * HEAD_DIM
IN_AB = 3 * W_SB + 4 * W_RET
OUT_AB = W_SB + W_RET
W_Q_SWA = N_HEADS_SWA * HEAD_DIM
W_KV_SWA = N_KV_SWA * HEAD_DIM
IN_C = W_Q_SWA + 2 * W_KV_SWA
N_EVEN = (DEPTH + 1) // 2
N_ODD = DEPTH // 2

kernel_name = 'hybrid_sb_retnet_swa_hmoe'

def rms_norm(x, g):
    xf = x.astype(jnp.float32)
    y = xf * lax.rsqrt(jnp.mean(jnp.square(xf), axis=-1, keepdims=True) + EPS)
    return (y * g.astype(jnp.float32)).astype(x.dtype)

def rope_tables(seq):
    pos = jnp.arange(seq, dtype=jnp.float32)
    inv = ROPE_THETA ** (-jnp.arange(0, HEAD_DIM, 2, dtype=jnp.float32) / HEAD_DIM)
    ang = pos[:, None] * inv[None, :]
    return jnp.cos(ang), jnp.sin(ang)

def apply_rope(x, cos, sin):
    half = x.shape[-1] // 2
    xf = x.astype(jnp.float32)
    x1, x2 = xf[..., :half], xf[..., half:]
    c = cos[None, :, None, :]
    s = sin[None, :, None, :]
    return jnp.concatenate([x1 * c - x2 * s, x2 * c + x1 * s], axis=-1).astype(x.dtype)

def stick_breaking_attention(q, k, v):
    B, S, H, d = q.shape
    scale = d ** -0.5
    outs = []
    for start in range(0, S, Q_BLOCK):
        end = start + Q_BLOCK
        qb = q[:, start:end]
        kb = k[:, :end]
        vb = v[:, :end]
        z = jnp.einsum('bqhd,bkhd->bhqk', qb, kb).astype(jnp.float32) * scale
        qpos = start + jnp.arange(Q_BLOCK)
        kpos = jnp.arange(end)
        strict = kpos[None, :] < qpos[:, None]
        log_fail = jnp.where(strict, jax.nn.log_sigmoid(-z), 0.0)
        after = lax.cumsum(log_fail, axis=3, reverse=True) - log_fail
        w = jnp.where(strict, jnp.exp(jax.nn.log_sigmoid(z) + after), 0.0)
        outs.append(jnp.einsum('bhqk,bkhd->bqhd', w.astype(vb.dtype), vb))
    return jnp.concatenate(outs, axis=1)

def retention_chunkwise(q, k, v):
    B, S, H, d = q.shape
    C = RET_CHUNK
    n = S // C
    q = q.astype(jnp.float32)
    k = k.astype(jnp.float32) * (d ** -0.5)
    v = v.astype(jnp.float32)
    log_g = jnp.log(1.0 - 2.0 ** (-5.0 - jnp.arange(H, dtype=jnp.float32)))
    idx = jnp.arange(C, dtype=jnp.float32)
    diff = idx[:, None] - idx[None, :]
    decay_in = jnp.where(diff[None] >= 0, jnp.exp(log_g[:, None, None] * jnp.maximum(diff, 0.0)[None]), 0.0)
    xi = jnp.exp(log_g[:, None] * (idx[None, :] + 1.0))
    zeta = jnp.exp(log_g[:, None] * (C - 1.0 - idx[None, :]))
    g_chunk = jnp.exp(log_g * C)

    def to_chunks(t):
        return t.reshape(B, n, C, H, d).transpose(1, 0, 3, 2, 4)

    def step(R, inp):
        qi, ki, vi = inp
        inner = jnp.einsum('bhqd,bhkd->bhqk', qi, ki) * decay_in[None]
        o = jnp.einsum('bhqk,bhke->bhqe', inner, vi) + jnp.einsum('bhqd,bhde->bhqe', qi, R) * xi[None, :, :, None]
        R = R * g_chunk[None, :, None, None] + jnp.einsum('bhkd,bhke->bhde', ki * zeta[None, :, :, None], vi)
        return R, o

    R0 = jnp.zeros((B, H, d, d), jnp.float32)
    _, o = lax.scan(step, R0, (to_chunks(q), to_chunks(k), to_chunks(v)))
    return o.transpose(1, 0, 3, 2, 4).reshape(B, S, H, d)

def head_group_norm(y, gain):
    B, S, H, d = y.shape
    mu = jnp.mean(y, axis=-1, keepdims=True)
    var = jnp.mean(jnp.square(y - mu), axis=-1, keepdims=True)
    yn = (y - mu) * lax.rsqrt(var + EPS)
    return yn.reshape(B, S, H * d) * gain.astype(jnp.float32)

def sliding_window_gqa_sinks(q, k, v, sinks):
    B, S, Hq, d = q.shape
    Hkv = k.shape[2]
    G = Hq // Hkv
    W = WINDOW
    nb = S // W
    qb = q.reshape(B, nb, W, Hkv, G, d)

    def band(t):
        tp = jnp.pad(t, ((0, 0), (W, 0), (0, 0), (0, 0))).reshape(B, nb + 1, W, Hkv, d)
        return jnp.concatenate([tp[:, :-1], tp[:, 1:]], axis=2)

    kband, vband = band(k), band(v)
    s = jnp.einsum('bnqhgd,bnkhd->bnhgqk', qb, kband).astype(jnp.float32) * (d ** -0.5)
    qi = jnp.arange(W)[:, None]
    kj = jnp.arange(2 * W)[None, :]
    rel = qi + W - kj
    local = (rel >= 0) & (rel < W)
    blk = jnp.arange(nb)[:, None, None]
    valid = local[None] & ((blk > 0) | (kj[None] >= W))
    s = jnp.where(valid[None, :, None, None], s, -jnp.inf)
    sink = sinks.astype(jnp.float32).reshape(Hkv, G)[None, None, :, :, None, None]
    m = jnp.maximum(jnp.max(s, axis=-1, keepdims=True), sink)
    p = jnp.exp(s - m)
    p = p / (jnp.sum(p, axis=-1, keepdims=True) + jnp.exp(sink - m))
    o = jnp.einsum('bnhgqk,bnkhd->bnqhgd', p.astype(vband.dtype), vband)
    return o.reshape(B, S, Hq, d)

def mixer_ab(hn, w_in, gn_gain, w_out, cos, sin):
    B, S, _ = hn.shape
    proj = hn @ w_in
    cuts = list(np.cumsum([W_SB, W_SB, W_SB, W_RET, W_RET, W_RET])[:])
    qa, ka, va, qr, kr, vr, gr = jnp.split(proj, cuts, axis=-1)
    heads = lambda t, h: t.reshape(B, S, h, HEAD_DIM)
    a = stick_breaking_attention(heads(qa, N_HEADS_SB), heads(ka, N_HEADS_SB), heads(va, N_HEADS_SB))
    r = retention_chunkwise(apply_rope(heads(qr, N_HEADS_RET), cos, sin),
                            apply_rope(heads(kr, N_HEADS_RET), cos, sin),
                            heads(vr, N_HEADS_RET))
    r = head_group_norm(r, gn_gain) * jax.nn.silu(gr.astype(jnp.float32))
    cat = jnp.concatenate([a.reshape(B, S, W_SB), r.astype(a.dtype)], axis=-1)
    return cat @ w_out

def mixer_c(hn, w_in, b_in, sinks, w_out, b_out, cos, sin):
    B, S, _ = hn.shape
    proj = hn @ w_in + b_in
    q, k, v = jnp.split(proj, [W_Q_SWA, W_Q_SWA + W_KV_SWA], axis=-1)
    q = apply_rope(q.reshape(B, S, N_HEADS_SWA, HEAD_DIM), cos, sin)
    k = apply_rope(k.reshape(B, S, N_KV_SWA, HEAD_DIM), cos, sin)
    v = v.reshape(B, S, N_KV_SWA, HEAD_DIM)
    o = sliding_window_gqa_sinks(q, k, v, sinks)
    return o.reshape(B, S, W_Q_SWA) @ w_out + b_out

def hierarchical_moe(x, w_group, w_expert_router, w_gate, w_up, w_down):
    B, S, D = x.shape
    N = B * S
    M = MOE_BLOCK
    xf = x.reshape(N, D)
    group_probs = jax.nn.softmax((xf @ w_group).astype(jnp.float32), axis=-1)
    g_prob, g_idx = lax.top_k(group_probs, 1)
    e_logits = (xf @ w_expert_router).astype(jnp.float32).reshape(N, N_GROUPS, EXPERTS_PER_GROUP)
    e_logits = e_logits[jnp.arange(N), g_idx[:, 0]]
    e_prob, e_idx = lax.top_k(jax.nn.softmax(e_logits, axis=-1), TOP_K_IN_GROUP)
    e_prob = e_prob / jnp.sum(e_prob, axis=-1, keepdims=True)
    gate = (g_prob * e_prob).reshape(-1)
    eid = (g_idx * EXPERTS_PER_GROUP + e_idx).reshape(-1).astype(jnp.int32)
    tok = jnp.repeat(jnp.arange(N, dtype=jnp.int32), TOP_K_IN_GROUP)
    P = N * TOP_K_IN_GROUP
    order = jnp.argsort(eid)
    s_eid, s_tok, s_w = eid[order], tok[order], gate[order]
    counts = jnp.bincount(eid, length=N_EXPERTS).astype(jnp.int32)
    padded = ((counts + M - 1) // M) * M
    start = jnp.cumsum(counts) - counts
    pend = jnp.cumsum(padded)
    pstart = pend - padded
    dest = pstart[s_eid] + jnp.arange(P, dtype=jnp.int32) - start[s_eid]
    R = P + N_EXPERTS * M
    nblk = R // M
    row_tok = jnp.zeros((R,), jnp.int32).at[dest].set(s_tok)
    row_w = jnp.zeros((R,), s_w.dtype).at[dest].set(s_w)
    blk_exp = jnp.minimum(jnp.searchsorted(pend, jnp.arange(nblk, dtype=jnp.int32) * M, side='right'), N_EXPERTS - 1)
    xs = xf[row_tok].reshape(nblk, M, D)

    def expert_block(args):
        xb, e = args
        h = jax.nn.silu(xb @ w_gate[e]) * (xb @ w_up[e])
        return h @ w_down[e]

    ys = lax.map(expert_block, (xs, blk_exp)).reshape(R, D)
    y = jnp.zeros((N, D), ys.dtype).at[row_tok].add(ys * row_w[:, None].astype(ys.dtype))
    return y.reshape(B, S, D)

def setup_inputs(seed: int = 0) -> dict:
    key = jax.random.key(seed)
    ks = jax.random.split(key, 20)
    f32 = jnp.float32
    nrm = lambda k, shape, fan_in: jax.random.normal(k, shape, f32) * (fan_in ** -0.5)
    return {
        'x': jax.random.normal(ks[0], (BATCH, SEQ, D_MODEL), f32),
        'attn_norm_g': 1.0 + 0.02 * jax.random.normal(ks[1], (DEPTH, D_MODEL), f32),
        'ffn_norm_g': 1.0 + 0.02 * jax.random.normal(ks[2], (DEPTH, D_MODEL), f32),
        'w_in_ab': nrm(ks[3], (N_EVEN, D_MODEL, IN_AB), D_MODEL),
        'w_out_ab': nrm(ks[4], (N_EVEN, OUT_AB, D_MODEL), OUT_AB),
        'ret_gn_g': 1.0 + 0.02 * jax.random.normal(ks[5], (N_EVEN, W_RET), f32),
        'w_in_c': nrm(ks[6], (N_ODD, D_MODEL, IN_C), D_MODEL),
        'b_in_c': 0.02 * jax.random.normal(ks[7], (N_ODD, IN_C), f32),
        'sinks': 0.5 * jax.random.normal(ks[8], (N_ODD, N_HEADS_SWA), f32),
        'w_out_c': nrm(ks[9], (N_ODD, W_Q_SWA, D_MODEL), W_Q_SWA),
        'b_out_c': 0.02 * jax.random.normal(ks[10], (N_ODD, D_MODEL), f32),
        'w_group': nrm(ks[11], (DEPTH, D_MODEL, N_GROUPS), D_MODEL),
        'w_expert_router': nrm(ks[12], (DEPTH, D_MODEL, N_EXPERTS), D_MODEL),
        'w_gate': nrm(ks[13], (DEPTH, N_EXPERTS, D_MODEL, D_EXPERT), D_MODEL),
        'w_up': nrm(ks[14], (DEPTH, N_EXPERTS, D_MODEL, D_EXPERT), D_MODEL),
        'w_down': nrm(ks[15], (DEPTH, N_EXPERTS, D_EXPERT, D_MODEL), D_EXPERT),
        'final_norm_g': 1.0 + 0.02 * jax.random.normal(ks[16], (D_MODEL,), f32),
    }

def reference(x, attn_norm_g, ffn_norm_g, w_in_ab, w_out_ab, ret_gn_g, w_in_c, b_in_c, sinks,
              w_out_c, b_out_c, w_group, w_expert_router, w_gate, w_up, w_down, final_norm_g):
    S = x.shape[1]
    cos, sin = rope_tables(S)
    h = x
    for layer in range(DEPTH):
        i = layer // 2
        hn = rms_norm(h, attn_norm_g[layer])
        if layer % 2 == 0:
            mix = mixer_ab(hn, w_in_ab[i], ret_gn_g[i], w_out_ab[i], cos, sin)
        else:
            mix = mixer_c(hn, w_in_c[i], b_in_c[i], sinks[i], w_out_c[i], b_out_c[i], cos, sin)
        h = h + mix.astype(h.dtype)
        ff = hierarchical_moe(rms_norm(h, ffn_norm_g[layer]), w_group[layer], w_expert_router[layer],
                              w_gate[layer], w_up[layer], w_down[layer])
        h = h + ff.astype(h.dtype)
    return rms_norm(h, final_norm_g)


_drawn_inputs = setup_inputs


def setup_inputs(seed=0):
    import zlib

    import numpy as np

    out = dict(_drawn_inputs(seed))
    spreads = {}
    factors = {'sinks': 4.896, 'final_norm_g': 2.864}
    for name, (base, spread) in spreads.items():
        noise = np.random.default_rng([zlib.crc32(name.encode()), seed]).standard_normal(out[name].shape)
        drawn = base * np.exp(spread * noise) if base else spread * noise
        out[name] = __import__('jax').numpy.asarray(drawn.astype(out[name].dtype))
    for name, factor in factors.items():
        out[name] = (out[name] * factor).astype(out[name].dtype)
    return out
```

```python
from contextlib import ExitStack

import numpy as np

import concourse.bass as bass
from concourse import mybir

F32 = mybir.dt.float32
I32 = mybir.dt.int32
ALU = mybir.AluOpType
ACT = mybir.ActivationFunctionType
AX_X = mybir.AxisListType.X

P = 128
D = 1024
S = 256
NB = S // P
KD = D // P
HD = 64
HALF = 512
DEPTH = 2

SB_HEADS = 8
SB_GROUPS = SB_HEADS // 2
RET_HEADS = 8
TRI = 384
AB_IN = 7
AB_UNITS = AB_IN + 2

SWA_HEADS = 16
KV_HEADS = 4
C_IN = 3
C_UNITS = C_IN + 2

EXPERTS = 32
GROUPS = 4
PER_GROUP = EXPERTS // GROUPS
DE = 512
MH = DE // P
CAP = 64
PASSES = S // CAP
PAIRS = EXPERTS // 2
ROUTER = GROUPS + EXPERTS

RING = 6
UNIT = 4096
EPS = 1e-6
BIG = 1e30

EARLY = {"ident": 128, "before": 128, "neg_from": 128, "cos": NB * HD, "sin": NB * HD}
LATE = {"decay": RET_HEADS * S, "swa_mask": TRI, "slots": CAP, "first4": GROUPS, "first8": PER_GROUP}


def constant_tables():
    f32 = np.float32
    p, c = np.arange(P)[:, None], np.arange(P)[None, :]
    before = (p < c).astype(f32)
    inv = f32(10000.0) ** (-np.arange(0, HD, 2, dtype=f32) / f32(HD))
    ang = np.arange(S, dtype=f32)[:, None] * inv[None, :]
    cos, sin = np.cos(ang), np.sin(ang)
    cos2 = np.concatenate([cos, cos], 1).reshape(NB, P, HD).transpose(1, 0, 2).reshape(P, -1)
    sin2 = np.concatenate([-sin, sin], 1).reshape(NB, P, HD).transpose(1, 0, 2).reshape(P, -1)
    early = np.concatenate([np.eye(P, dtype=f32), before, before - 1, cos2, sin2], 1)
    log_g = np.log(f32(1.0) - f32(2.0) ** (f32(-5.0) - np.arange(RET_HEADS, dtype=f32)))
    ahead = np.arange(S, dtype=f32)[None, None, :] - np.arange(P, dtype=f32)[:, None, None]
    decay = np.where(ahead >= 0, np.exp(log_g[None, :, None] * np.maximum(ahead, 0)), 0) * HD ** -0.5
    diag = np.where(c <= p, 0, BIG)
    swa = np.concatenate([diag, np.where(c > p, 0, BIG), diag], 1)
    row = np.concatenate([np.arange(CAP), np.arange(GROUPS, 0, -1), np.arange(PER_GROUP, 0, -1)])
    late = np.concatenate([decay.reshape(P, -1), swa, np.tile(row, (P, 1))], 1)
    return early.astype(f32), late.astype(f32)


def hybrid_trunk(nc, x, attn_norm_g, ffn_norm_g, w_in_ab, w_out_ab, ret_gn_g, w_in_c, b_in_c, sinks,
                 w_out_c, b_out_c, w_group, w_expert_router, w_gate, w_up, w_down, final_norm_g,
                 early_table, late_table, out):
    ctx = ExitStack()
    with ctx:
        ctx.enter_context(nc.allow_non_contiguous_dma(reason="small per-partition gains and router rows"))

        def sb(name, shape, dt=F32):
            return ctx.enter_context(nc.sbuf_tensor(name, shape, dt))

        def sem(name):
            return ctx.enter_context(nc.semaphore(name))

        ring = sb("ring", [P, RING, UNIT])
        h = sb("h", [P, NB, D])
        hr = sb("hr", [P, NB, KD, P])
        hnT = sb("hnT", [P, KD, S])
        early = sb("early", [P, sum(EARLY.values())])
        late = sb("late", [P, CAP + GROUPS + PER_GROUP + TRI])
        ones = sb("ones", [P, P])
        neg_ones = sb("neg_ones", [P, P])
        minus_half = sb("minus_half", [P, NB * RET_HEADS])
        gains = sb("gains", [P, 2 * DEPTH, KD])
        gn_gain = sb("gn_gain", [P, 4])
        sinks_b = sb("sinks_b", [P, SWA_HEADS])
        sink_neg = sb("sink_neg", [P, SWA_HEADS])
        router = sb("router", [P, DEPTH, KD, ROUTER])
        ms = sb("ms", [P, 2 * DEPTH + 1, NB])
        rstd = sb("rstd", [P, 2 * DEPTH + 1, NB])
        rank_all = sb("rank_all", [P, NB, PASSES * EXPERTS])
        gate_all = sb("gate_all", [P, NB, PASSES * EXPERTS])
        tmp = sb("tmp", [P, 800])
        rounds = sb("rounds", [1, DEPTH, 2], I32)
        arena = sb("arena", [P, 16800])

        pos = [0]

        def carve(*shape, at=None):
            n = int(np.prod(shape))
            lo = pos[0] if at is None else at
            if at is None:
                pos[0] += n
            assert lo + n <= 16800
            v = arena[:, lo:lo + n]
            if len(shape) == 2:
                v = v.rearrange("p (a b) -> p a b", a=shape[0])
            if len(shape) == 3:
                v = v.rearrange("p (a b c) -> p a b c", a=shape[0], b=shape[1])
            return v

        sb_qT, sb_kT, sb_v = carve(SB_GROUPS, S), carve(SB_GROUPS, S), carve(NB, HALF)
        sb_w = carve(4, TRI)
        r_q, r_k, r_v, r_gate = (carve(NB, HALF) for _ in range(4))
        rope_a, rope_b = carve(NB, HALF), carve(NB, HALF)
        r_w = carve(2, TRI)
        catT = carve(KD, S)
        decay = carve(RET_HEADS, S)
        r_qT = hnT[:, 0:4, :]
        r_kT = hnT[:, 4:8, :]
        r_c, r_sq = rope_a, rope_b
        pos[0] = 0
        c_q, c_k, c_v = carve(NB, D), carve(NB, KV_HEADS * 2 * HD), carve(NB, KV_HEADS * HD)
        c_in, c_a, c_b = carve(NB, HALF), carve(NB, HALF), carve(NB, HALF)
        c_kT = carve(KV_HEADS, S)
        c_s, c_p, c_pT = carve(2, TRI), carve(2, TRI), carve(2, TRI)
        c_o = carve(NB, D)
        c_min, c_sum, c_den = (carve(SWA_HEADS, NB) for _ in range(3))
        c_bin, c_bout = carve(C_IN * HALF), carve(D)
        c_qT = hnT
        attT = carve(KD, S, at=0)
        pos[0] = 0
        pick, pick_w = carve(NB, P), carve(NB, P)
        xeT = carve(KD, P)
        e_silu, e_h, e_hT = carve(DE), carve(DE), carve(MH, P)
        e_y = carve(D)
        pick_wT = carve(S)
        final_gain = carve(D, at=15700)

        spent = [0]

        def small(*shape):
            n = int(np.prod(shape))
            v = tmp[:, spent[0]:spent[0] + n]
            spent[0] += n
            if len(shape) == 2:
                v = v.rearrange("p (a b) -> p a b", a=shape[0])
            if len(shape) == 3:
                v = v.rearrange("p (a b c) -> p a b c", a=shape[0], b=shape[1])
            return v

        logits = small(NB, ROUTER)
        g_max, g_sum, g_prob, g_best = (small(NB) for _ in range(4))
        g_less, g_exp, g_score, g_hot = (small(NB, GROUPS) for _ in range(4))
        e_all = small(NB, GROUPS, PER_GROUP)
        e_log, e_less, e_score, e_hot1, e_rest, e_hot2 = (small(NB, PER_GROUP) for _ in range(6))
        e_max, e_best, e_max2, e_ratio, e_den, gate1, gate2 = (small(NB) for _ in range(7))
        e_gate1, e_gate2, e_gates, e_both = (small(NB, PER_GROUP) for _ in range(4))
        chosen, gates, rank = (small(NB, GROUPS, PER_GROUP) for _ in range(3))
        fullest, fullest_all = small(1), small(1)
        more = small(PASSES - 1)
        gn_sum, gn_rstd = small(NB, RET_HEADS), small(NB, RET_HEADS)

        spot = {}
        lo = 0
        for name, n in EARLY.items():
            spot[name] = early[:, lo:lo + n]
            lo += n
        ident, before, neg_from = spot["ident"], spot["before"], spot["neg_from"]
        cos = spot["cos"].rearrange("p (b c) -> p b c", b=NB)
        sin = spot["sin"].rearrange("p (b c) -> p b c", b=NB)
        swa_mask = late[:, 0:TRI]
        slots = late[:, TRI:TRI + CAP]
        first4 = late[:, TRI + CAP:TRI + CAP + GROUPS]
        first8 = late[:, TRI + CAP + GROUPS:TRI + CAP + GROUPS + PER_GROUP]

        bank = [ctx.enter_context(nc.psum_tensor(f"bank{i}", [P, HALF], F32)) for i in range(8)]

        x_in, early_in, late_in = sem("x_in"), sem("early_in"), sem("late_in")
        small_in, bias_in = sem("small_in"), sem("bias_in")
        ones_set = sem("ones_set")
        dve_step, act_step, pool_step = sem("dve_step"), sem("act_step"), sem("pool_step")
        squares = sem("squares")
        rooted = sem("rooted")
        rms_done = sem("rms_done")
        turned = sem("turned")
        normed = sem("normed")
        h_done = sem("h_done")
        out_ready = sem("out_ready")
        out_done = sem("out_done")
        ab = {n: sem("ab_" + n) for n in (
            "used", "act_evac", "rope_mul", "roped", "z", "log1p", "softplus", "cum", "expw",
            "weights", "av", "cat", "rq_turned", "rk_turned", "rq", "rk", "inner", "decayed", "ret_o",
            "gn", "gn_var", "gn_root", "gn_turned", "gn_cat", "out")}
        ab_landed = [sem(f"ab_landed{i}") for i in range(RING)]
        cc = {n: sem("c_" + n) for n in (
            "used", "biased", "rope_swap", "roped", "k_turned", "k", "q_turned", "q", "scores", "masked",
            "prob", "sink", "sink_exp", "p_turned", "pT", "o", "o_norm", "o_turned", "att_act", "att_dve",
            "out", "bias_h")}
        c_landed = [sem(f"c_landed{i}") for i in range(C_UNITS)]
        moe = []
        for l in range(DEPTH):
            m = {n: sem(f"m{l}_{n}") for n in (
                "logits", "group_less", "group_exp", "second", "second_exp", "chosen", "ranked", "fullest",
                "fullest_row", "rounds", "gathered", "xe", "silu", "hidden", "h_turned", "hT",
                "pickT", "pickT_sb", "y_low", "y_high", "pick", "pick_w", "used", "combined")}
            m["landed"] = [sem(f"m{l}_landed{i}") for i in range(RING)]
            moe.append(m)

        x_v = x[0].rearrange("(b p) d -> p b d", p=P)
        out_v = out[0].rearrange("(b p) d -> p b d", p=P)
        w_ab_v = w_in_ab[0].rearrange("(p k) n -> p k n", k=KD)
        w_c_v = w_in_c[0].rearrange("(p k) n -> p k n", k=KD)
        wo_ab_v = w_out_ab[0].rearrange("(u c p) n -> u p c n", u=2, p=P)
        wo_c_v = w_out_c[0].rearrange("(u c p) n -> u p c n", u=2, p=P)
        C_COLS = [2 * HALF, 0, HALF]
        OUT_BANKS = [0, 1, 6, 7]

        def slot_in(s):
            return ring[:, s, :].rearrange("p (k n) -> p k n", k=KD)

        def slot_out(s):
            return ring[:, s, :].rearrange("p (c n) -> p c n", c=4)

        def flat(v):
            return v.rearrange("p a b -> p (a b)")

        def row_bcast(v, n):
            return bass.AP(v.tensor, v.offset, [[0, P], [1, n]])

        def per_head(v, heads):
            return v.rearrange("p (h a c) -> p h a c", h=heads, a=2)

        def swapped(v, heads):
            ps, pn = v.ap[0]
            return bass.AP(v.tensor, v.offset + HD // 2, [[ps, pn], [HD, heads], [-HD // 2, 2], [1, HD // 2]])

        def over_heads(v, heads):
            ps, pn = v.ap[0]
            return bass.AP(v.tensor, v.offset, [[ps, pn], [0, heads], [HD // 2, 2], [1, HD // 2]])

        def spread(v, n):
            return v.unsqueeze(len(v.shape)).broadcast_to([*v.shape, n])

        def diagonal(v):
            return v.rearrange("p (a c) -> p a c", a=3)[:, 0:3:2, :]

        def of_block(t, b):
            return t[:, b * P:(b + 1) * P]

        def pair_rows(t):
            return t.rearrange("p b (s c) -> p b s c", s=2)

        def of_pair(t, i):
            return spread(t[:, :, bass.ds(2 * i, 2)], CAP)

        before2 = before.unsqueeze(1).broadcast_to([P, 2, P])

        def head_rows(t, head, chunk=None):
            off = (head % 2) * HD
            return t[off:off + HD, head // 2 if chunk is None else chunk, :]

        block = ctx.enter_context(nc.Block())

        @block.sync
        def _(sp):
            def expert_unit(l, e, kind):
                one = bass.ds(e, 1)
                if kind < 2:
                    return (w_gate, w_up)[kind][l, one].rearrange("a (p k) n -> p (a k) n", k=KD)
                return w_down[l, one].rearrange("a (m p) n -> p (a m) n", p=P)

            def expert_slot(j):
                return slot_in(j) if j < 4 else slot_out(j)

            def experts(l, slot_free):
                m = moe[l]
                for j in range(RING):
                    slot_free(j)
                    sp.dma_start(expert_slot(j), expert_unit(l, j % 2, j // 2)).then_inc(m["landed"][j], 16)
                sp.wait_ge(m["rounds"], 1)
                last = sp.value_load(rounds[0:1, l, 1:2], min_val=PAIRS - 1, max_val=PAIRS * PASSES - 1)
                with sp.Fori(0, last) as i:
                    for j in range(RING):
                        e = ((i + 1) % PAIRS) * 2 + j % 2
                        sp.compute_val(e * (D * DE) * 4)
                        sp.wait_ge(m["used"], 3 * i + (j // 2 + 1))
                        sp.dma_start(expert_slot(j), expert_unit(l, e, j // 2)).then_inc(m["landed"][j], 16)
                return last

            sp.dma_start(h[:], x_v).then_inc(x_in, 16)
            for u in range(AB_UNITS):
                s = u % RING
                if u >= RING:
                    sp.wait_ge(ab["used"], u - RING + 1)
                if u < AB_IN:
                    sp.dma_start(slot_in(s), w_ab_v[:, :, u * HALF:(u + 1) * HALF]).then_inc(ab_landed[s], 16)
                else:
                    sp.dma_start(slot_out(s), wo_ab_v[u - AB_IN]).then_inc(ab_landed[s], 16)

            def after_ab(j):
                sp.wait_ge(ab["used"], (j if j + RING >= AB_UNITS else j + RING) + 1)

            def after_c(j):
                if j < C_UNITS:
                    sp.wait_ge(cc["used"], j + 1)

            last = experts(0, after_ab)
            for u in range(C_UNITS):
                sp.wait_ge(moe[0]["used"], 3 * last + (u // 2 + 1))
                if u < C_IN:
                    sp.dma_start(slot_in(u), w_c_v[:, :, C_COLS[u]:C_COLS[u] + HALF]).then_inc(c_landed[u], 16)
                else:
                    sp.dma_start(slot_out(u), wo_c_v[u - C_IN]).then_inc(c_landed[u], 16)
            experts(1, after_c)
            for b in range(NB):
                sp.wait_ge(out_ready, b + 1)
                sp.dma_start(out_v[:, b, :], hr[:, b].rearrange("p k c -> p (k c)")).then_inc(out_done, 16)
            sp.wait_ge(out_done, 16 * NB)

        @block.gpsimd
        def _(pool):
            steps = [0]

            def link(op):
                steps[0] += 1
                op.then_inc(pool_step, 1)
                pool.wait_ge(pool_step, steps[0])

            link(pool.memset(minus_half[:], -0.5))
            pool.memset(ones[:], 1.0).then_inc(ones_set, 1)
            pool.memset(neg_ones[:], -1.0).then_inc(ones_set, 1)

            def inverse_rms(n):
                for b in range(NB):
                    pool.wait_ge(squares, NB * n + b + 1)
                    link(pool.tensor_scalar(rstd[:, n, b:b + 1], ms[:, n, b:b + 1], EPS, None, ALU.add))
                    pool.tensor_tensor(rstd[:, n, b:b + 1], rstd[:, n, b:b + 1], minus_half[:, 0:1],
                                       ALU.pow).then_inc(rooted, 1)

            inverse_rms(0)
            for v, dst in enumerate((r_q, r_k)):
                pool.wait_ge(ab["rope_mul"], v + 1)
                pool.tensor_tensor(flat(dst), flat(rope_a), flat(rope_b), ALU.add).then_inc(ab["roped"], 1)

            def experts(l):
                m = moe[l]

                def weighted(i):
                    pool.tensor_tensor(pair_rows(pick_w), pair_rows(pick), of_pair(gate_all, i),
                                       ALU.mult).then_inc(m["pick_w"], 1)

                pool.wait_ge(m["pick"], 1)
                weighted(0)
                pool.wait_ge(m["rounds"], 1)
                n = pool.value_load(rounds[0:1, l, 0:1], min_val=PAIRS, max_val=PAIRS * PASSES)
                with pool.Fori(1, n) as i:
                    pool.wait_ge(m["pick"], i + 1)
                    pool.wait_ge(m["pickT"], i)
                    weighted(i)

            pool.wait_ge(ab["gn_var"], 1)
            link(pool.tensor_scalar(flat(gn_rstd), flat(gn_sum), HD * EPS, None, ALU.add))
            pool.tensor_tensor(flat(gn_rstd), flat(gn_rstd), minus_half[:], ALU.pow).then_inc(ab["gn_root"], 1)
            inverse_rms(1)
            experts(0)
            inverse_rms(2)
            for u in range(C_IN):
                heads = SB_HEADS if u else KV_HEADS
                pool.wait_ge(cc["biased"], u + 1)
                if u:
                    pool.wait_ge(cc["roped"], u)
                for b in range(NB):
                    op = pool.tensor_tensor(per_head(c_b[:, b, 0:heads * HD], heads),
                                            swapped(c_in[:, b, 0:heads * HD], heads),
                                            over_heads(sin[:, b, :], heads), ALU.mult)
                op.then_inc(cc["rope_swap"], 1)
            pool.wait_ge(bias_in, 48)
            for b in range(NB):
                op = pool.tensor_tensor(h[:, b, :], h[:, b, :], c_bout, ALU.add)
            op.then_inc(cc["bias_h"], 1)
            inverse_rms(3)
            experts(1)
            inverse_rms(4)

        @block.scalar
        def _(act):
            steps = [0]

            def link(op):
                steps[0] += 1
                op.then_inc(act_step, 1)
                act.wait_ge(act_step, steps[0])

            act.dma_start(early[:], early_table).then_inc(early_in, 16)
            for l in range(DEPTH):
                for j, g in ((0, attn_norm_g), (1, ffn_norm_g)):
                    act.dma_start(gains[:, 2 * l + j, :], g[l].rearrange("(p k) -> p k", k=KD)).then_inc(small_in, 16)
                act.dma_start(router[:, l, :, 0:GROUPS],
                              w_group[l].rearrange("(p k) n -> p k n", k=KD)).then_inc(small_in, 16)
                act.dma_start(router[:, l, :, GROUPS:ROUTER],
                              w_expert_router[l].rearrange("(p k) n -> p k n", k=KD)).then_inc(small_in, 16)
            act.dma_start(gn_gain[:], ret_gn_g[0].rearrange("(c p) -> p c", p=P)).then_inc(small_in, 16)
            act.dma_start(sinks_b[:], row_bcast(sinks, SWA_HEADS)).then_inc(small_in, 16)
            act.dma_start(flat(decay), late_table[:, 0:RET_HEADS * S]).then_inc(late_in, 16)
            act.dma_start(late[:], late_table[:, RET_HEADS * S:]).then_inc(late_in, 16)

            def mean_squares(n):
                for b in range(NB):
                    if n == 0:
                        act.wait_ge(x_in, 16)
                    else:
                        act.wait_ge(h_done, NB * (n - 1) + b + 1)
                    act.activation(flat(hr[:, b]), h[:, b, :], ACT.Square, scale=D ** -0.5,
                                   accum_out=ms[:, n, b:b + 1]).then_inc(squares, 1)

            mean_squares(0)

            def evac(u, dst, func, scale):
                act.wait_ge(ab["used"], u + 1)
                for j in range(2):
                    op = act.activation(dst[j], bank[2 * (u % 2) + j][:], func, scale=scale)
                op.then_inc(ab["act_evac"], 1)

            def chunks(t):
                return [flat(t[:, 2 * j:2 * j + 2, :]) for j in range(2)]

            def blocks(t):
                return [t[:, b, :] for b in range(NB)]

            def log1p(g):
                act.wait_ge(ab["z"], g + 1)
                for s in range(2):
                    t = sb_w[:, 2 * (g % 2) + s, :]
                    link(act.activation(t, bank[4 + 2 * (g % 2) + s][:, 0:TRI], ACT.Abs))
                    link(act.activation(t, t, ACT.Exp, scale=-1.0))
                    act.activation(t, t, ACT.Ln, bias=1.0).then_inc(ab["log1p"], 1)

            def stick_weights(g):
                act.wait_ge(ab["cum"], g + 1)
                for s in range(2):
                    act.activation(sb_w[:, 2 * (g % 2) + s, :], bank[4 + 2 * (g % 2) + s][:, 0:TRI],
                                   ACT.Exp).then_inc(ab["expw"], 1)

            evac(0, chunks(sb_qT), ACT.Copy, HD ** -0.5)
            evac(1, chunks(sb_kT), ACT.Copy, 1.0)
            evac(2, blocks(sb_v), ACT.Copy, 1.0)
            log1p(0)
            stick_weights(0)
            log1p(1)
            stick_weights(1)
            log1p(2)
            evac(5, blocks(r_v), ACT.Copy, 1.0)
            stick_weights(2)
            log1p(3)
            stick_weights(3)
            evac(6, blocks(r_gate), ACT.Silu, 1.0)
            act.wait_ge(ab["rk_turned"], 1)
            for j in range(2):
                op = act.activation(flat(r_kT[:, 2 * j:2 * j + 2, :]), bank[4 + j][:], ACT.Copy)
            op.then_inc(ab["rk"], 1)

            def experts(l):
                m = moe[l]
                act.wait_ge(m["group_less"], 1)
                act.activation(g_exp, g_less, ACT.Exp).then_inc(m["group_exp"], 1)
                act.wait_ge(m["second"], 1)
                act.activation(e_ratio, e_max2, ACT.Exp).then_inc(m["second_exp"], 1)

                def silu(i, first=False):
                    act.wait_ge(m["used"], 3 * i + 1)
                    if not first:
                        act.wait_ge(m["hidden"], i)
                    act.activation(e_silu, bank[6][:], ACT.Silu).then_inc(m["silu"], 1)

                def copy_hidden(i):
                    act.wait_ge(m["h_turned"], i + 1)
                    act.activation(flat(e_hT), bank[6][:], ACT.Copy).then_inc(m["hT"], 1)

                def copy_last(i):
                    act.wait_ge(m["used"], 3 * i)
                    act.activation(e_y[:, HALF:D], bank[5][:], ACT.Copy).then_inc(m["y_high"], 1)
                    act.wait_ge(m["pickT"], i)
                    act.activation(pick_wT, bank[7][:, 0:S], ACT.Copy).then_inc(m["pickT_sb"], 1)

                silu(0, first=True)
                copy_hidden(0)
                act.wait_ge(m["rounds"], 1)
                n = act.value_load(rounds[0:1, l, 0:1], min_val=PAIRS, max_val=PAIRS * PASSES)
                with act.Fori(1, n) as i:
                    copy_last(i)
                    silu(i)
                    copy_hidden(i)
                copy_last(n)

            mean_squares(1)
            act.dma_start(c_bin, row_bcast(b_in_c, C_IN * HALF)).then_inc(bias_in, 16)
            act.dma_start(c_bout, row_bcast(b_out_c, D)).then_inc(bias_in, 16)
            act.dma_start(final_gain, row_bcast(final_norm_g, D)).then_inc(bias_in, 16)
            experts(0)

            mean_squares(2)

            def turn_in(done, n, dst, banks, scale, signal):
                act.wait_ge(done, n)
                for j in range(2):
                    op = act.activation(flat(dst[:, 2 * j:2 * j + 2, :]), bank[banks[j]][:], ACT.Copy, scale=scale)
                op.then_inc(signal, 1)

            def prob(t):
                act.wait_ge(cc["masked"], t + 1)
                if t >= 2:
                    act.wait_ge(cc["p_turned"], t - 1)
                for b, cols in enumerate((slice(0, P), slice(P, TRI))):
                    op = act.activation(c_p[:, t % 2, cols], c_s[:, t % 2, cols], ACT.Exp, scale=-1.0,
                                        bias=c_min[:, t, b:b + 1], accum_out=c_sum[:, t, b:b + 1])
                op.then_inc(cc["prob"], 1)
                if t % 4 == 3:
                    act.wait_ge(cc["sink"], t // 4 + 1)
                    act.activation(c_den[:, t - 3:t + 1, :], c_den[:, t - 3:t + 1, :],
                                   ACT.Exp).then_inc(cc["sink_exp"], 1)

            turn_in(cc["k_turned"], 1, c_kT, (6, 7), 1.0, cc["k"])
            turn_in(cc["q_turned"], 1, c_qT[:, 0:4, :], (4, 5), -(HD ** -0.5), cc["q"])
            for t in range(SWA_HEADS):
                if t == 6:
                    turn_in(cc["q_turned"], 2, c_qT[:, 4:8, :], (2, 3), -(HD ** -0.5), cc["q"])
                prob(t)
            for b in range(NB):
                act.wait_ge(cc["o_turned"], 2 * b + 2)
                act.activation(attT[:, 4:8, b * P:(b + 1) * P], bank[3 + 2 * b][:].rearrange("p (c n) -> p c n", c=4),
                               ACT.Copy).then_inc(cc["att_act"], 1)
            mean_squares(3)
            experts(1)
            mean_squares(4)

        @block.tensor
        def _(pe):
            def turn(dst, src):
                return pe.transpose(dst, src, ident)

            def turn_normed(n):
                if n == 0:
                    pe.wait_ge(early_in, 16)
                for b in range(NB):
                    pe.wait_ge(rms_done, NB * n + b + 1)
                    for k in range(KD):
                        op = turn(of_block(bank[4 + 2 * b + k // 4], k % 4), hr[:, b, k, :])
                        if k % 4 == 3:
                            op.then_inc(turned, 1)
                pe.wait_ge(normed, 4 * (n + 1))

            def project(dst, unit):
                for b in range(NB):
                    for k in range(KD):
                        op = pe.matmul(dst[b][:], hnT[:, k, b * P:(b + 1) * P], unit[:, k, :],
                                       start=(k == 0), stop=(k == KD - 1))
                return op

            turn_normed(0)

            def in_proj(u):
                s = u % RING
                pe.wait_ge(ab_landed[s], 16 * (u // RING + 1))
                if u in (2, 3, 4):
                    pe.wait_ge(ab["act_evac"], u - 1)
                if u in (5, 6):
                    pe.wait_ge(ab["rope_mul"], u - 4)
                dst = bank[2 * (u % 2):2 * (u % 2) + 2]
                if u >= 2:
                    op = project(dst, slot_in(s))
                else:
                    for c in range(4):
                        for k in range(KD):
                            op = pe.matmul(dst[c // 2][:, (c % 2) * S:(c % 2 + 1) * S],
                                           slot_in(s)[:, k, c * P:(c + 1) * P], hnT[:, k, :],
                                           start=(k == 0), stop=(k == KD - 1))
                op.then_inc(ab["used"], 1)

            def triangle(dst, kT, qT):
                pe.matmul(dst[:, 0:S], kT[:, 0:P], qT, start=True, stop=True, skip_group_check=True)
                return pe.matmul(dst[:, S:TRI], kT[:, P:S], qT[:, P:S], start=False, stop=True,
                                 skip_group_check=True)

            def stick_scores(g):
                if g == 0:
                    pe.wait_ge(ab["act_evac"], 2)
                if g >= 2:
                    pe.wait_ge(ab["cat"], g - 1)
                for s in range(2):
                    head = 2 * g + s
                    op = triangle(bank[4 + 2 * (g % 2) + s], head_rows(sb_kT, head), head_rows(sb_qT, head))
                op.then_inc(ab["z"], 1)

            def stick_sums(g):
                pe.wait_ge(ab["softplus"], 2 * g + 2)
                if g == 0:
                    pe.wait_ge(ones_set, 2)
                for s in range(2):
                    dst, t = bank[4 + 2 * (g % 2) + s], sb_w[:, 2 * (g % 2) + s, :]
                    for cols, src, m in (((0, S), (0, S), neg_from), ((P, S), (S, TRI), neg_ones[:]),
                                         ((S, TRI), (S, TRI), neg_from)):
                        op = pe.matmul(dst[:, cols[0]:cols[1]], m, t[:, src[0]:src[1]], start=False, stop=True,
                                       skip_group_check=True)
                op.then_inc(ab["cum"], 1)

            def stick_values(g):
                pe.wait_ge(ab["weights"], 2 * g + 2)
                if g == 0:
                    pe.wait_ge(ab["act_evac"], 3)
                for s in range(2):
                    head = 2 * g + s
                    t = sb_w[:, 2 * (g % 2) + s, :]
                    rows = slice(s * HD, (s + 1) * HD)
                    v = [sb_v[:, b, head * HD:(head + 1) * HD] for b in range(NB)]
                    lo, hi = (bank[4 + 2 * (g % 2) + b][rows, TRI:HALF] for b in range(NB))
                    pe.matmul(lo, v[0], t[:, 0:P], start=True, stop=True)
                    pe.matmul(hi, v[0], t[:, P:S], start=True, stop=False)
                    op = pe.matmul(hi, v[1], t[:, S:TRI], start=False, stop=True)
                op.then_inc(ab["av"], 1)

            in_proj(0)
            in_proj(1)
            in_proj(2)
            stick_scores(0)
            in_proj(3)
            stick_sums(0)
            stick_scores(1)
            in_proj(4)
            stick_values(0)
            stick_sums(1)
            stick_scores(2)
            in_proj(5)
            stick_values(1)
            stick_sums(2)
            stick_scores(3)
            in_proj(6)
            stick_values(2)
            stick_sums(3)
            pe.wait_ge(ab["act_evac"], 4)
            pe.wait_ge(ab["roped"], 2)
            for c in range(4):
                for b in range(NB):
                    op = turn(bank[2 + c // 2][:, (c % 2) * S + b * P:(c % 2) * S + (b + 1) * P],
                              r_q[:, b, c * P:(c + 1) * P])
            op.then_inc(ab["rq_turned"], 1)
            pe.wait_ge(ab["cat"], 3)
            for c in range(4):
                for b in range(NB):
                    op = turn(bank[4 + c // 2][:, (c % 2) * S + b * P:(c % 2) * S + (b + 1) * P],
                              r_k[:, b, c * P:(c + 1) * P])
            op.then_inc(ab["rk_turned"], 1)
            stick_values(3)

            def inner(head):
                if head == 0:
                    pe.wait_ge(ab["rq"], 1)
                    pe.wait_ge(ab["rk"], 1)
                if head >= 2:
                    pe.wait_ge(ab["decayed"], head - 1)
                triangle(bank[2 + head % 2], head_rows(r_kT, head),
                         head_rows(r_qT, head)).then_inc(ab["inner"], 1)

            def ret_values(head):
                pe.wait_ge(ab["decayed"], head + 1)
                t = r_w[:, head % 2, :]
                cols = slice(head * HD, (head + 1) * HD)
                pe.matmul(bank[4][:, cols], t[:, 0:P], r_v[:, 0, cols], start=True, stop=True)
                pe.matmul(bank[5][:, cols], t[:, P:S], r_v[:, 0, cols], start=True, stop=False)
                pe.matmul(bank[5][:, cols], t[:, S:TRI], r_v[:, 1, cols], start=False,
                          stop=True).then_inc(ab["ret_o"], 1)

            inner(0)
            for head in range(1, RET_HEADS):
                inner(head)
                ret_values(head - 1)
            ret_values(RET_HEADS - 1)

            def out_proj(t, c, b, half, unit):
                return pe.matmul(bank[OUT_BANKS[2 * b + half]][:], t[:, c, b * P:(b + 1) * P],
                                 unit[:, c % 4, half * HALF:(half + 1) * HALF], start=(c == 0), stop=(c == KD - 1))

            pe.wait_ge(ab_landed[1], 32)
            pe.wait_ge(ab["act_evac"], 5)
            pe.wait_ge(ab["cat"], 4)
            for b in range(NB):
                for half in range(2):
                    for c in range(4):
                        op = out_proj(catT, c, b, half, slot_out(1))
            op.then_inc(ab["used"], 1)
            pe.wait_ge(ab["gn"], 1)
            for b in range(NB):
                for c in range(4):
                    op = turn(of_block(bank[2 + b], c), r_c[:, b, c * P:(c + 1) * P])
            op.then_inc(ab["gn_turned"], 1)
            pe.wait_ge(ab_landed[2], 32)
            pe.wait_ge(ab["gn_cat"], 1)
            for b in range(NB):
                for half in range(2):
                    for c in range(4, 8):
                        op = out_proj(catT, c, b, half, slot_out(2))
                op.then_inc(ab["out"] if b == 0 else ab["used"], 1)

            def experts(l):
                m = moe[l]
                pe.wait_ge(small_in, 160)
                for b in range(NB):
                    for k in range(KD):
                        op = pe.matmul(bank[0][:, b * CAP:b * CAP + ROUTER], hnT[:, k, b * P:(b + 1) * P],
                                       router[:, l, k, :], start=(k == 0), stop=(k == KD - 1))
                op.then_inc(m["logits"], 1)
                pe.wait_ge(m["chosen"], 1)
                one = [chosen[:, b].rearrange("p g e -> p (g e)") for b in range(NB)]
                pe.matmul(bank[1][:, 0:EXPERTS], before, one[0], start=True, stop=True)
                pe.matmul(bank[1][:, EXPERTS:2 * EXPERTS], before, one[1], start=True, stop=False)
                pe.matmul(bank[1][:, EXPERTS:2 * EXPERTS], ones[:], one[0], start=False,
                          stop=True).then_inc(m["ranked"], 1)

                def gather(i):
                    pe.wait_ge(m["pick"], i + 1)
                    for k in range(KD):
                        for b in range(NB):
                            op = pe.matmul(of_block(bank[4 + k // 4], k % 4), hr[:, b, k, :], pick[:, b, :],
                                           start=(b == 0), stop=(b == NB - 1))
                    op.then_inc(m["gathered"], 1)

                def both(i, kind, dst, lhsT, steps, cols):
                    for s in range(2):
                        pe.wait_ge(m["landed"][2 * kind + s], 16 * (i + 1))
                    unit = [(slot_out if kind == 2 else slot_in)(2 * kind + s) for s in range(2)]
                    for q in range(steps):
                        for s in range(2):
                            rows = slice(s * CAP, (s + 1) * CAP)
                            op = pe.matmul(dst[rows, :], lhsT[:, q, rows], unit[s][:, q, cols],
                                           start=(q == 0), stop=(q == steps - 1))
                    return op

                def turn_weights(i):
                    pe.wait_ge(m["pick_w"], i)
                    pe.wait_ge(m["hidden"], i)
                    for b in range(NB):
                        op = turn(of_block(bank[7], b), pick_w[:, b, :])
                    op.then_inc(m["pickT"], 1)

                def combine(i, first=False, last=False):
                    pe.wait_ge(m["y_low"], i)
                    pe.wait_ge(m["y_high"], i)
                    pe.wait_ge(m["pickT_sb"], i)
                    for b in range(NB):
                        for half in range(2):
                            op = pe.matmul(bank[2 * b + half][:], pick_wT[:, b * P:(b + 1) * P],
                                           e_y[:, half * HALF:(half + 1) * HALF], start=first, stop=last,
                                           skip_group_check=True)
                    if last:
                        op.then_inc(m["combined"], 1)

                def pair(i, first=False, second=False, final=False):
                    if not first:
                        turn_weights(i)
                    pe.wait_ge(m["xe"], i + 1)
                    if not first:
                        pe.wait_ge(m["hT"], i)
                    both(i, 0, bank[6], xeT, KD, slice(0, DE)).then_inc(m["used"], 1)
                    if not first:
                        pe.wait_ge(m["pickT_sb"], i)
                    both(i, 1, bank[7], xeT, KD, slice(0, DE)).then_inc(m["used"], 1)
                    if not first:
                        pe.wait_ge(m["y_low"], i)
                        pe.wait_ge(m["y_high"], i)
                    if not final:
                        gather(i + 1)
                    pe.wait_ge(m["hidden"], i + 1)
                    for mh in range(MH):
                        op = turn(of_block(bank[6], mh), e_h[:, mh * P:(mh + 1) * P])
                    op.then_inc(m["h_turned"], 1)
                    if not first:
                        combine(i, first=second)
                    pe.wait_ge(m["hT"], i + 1)
                    if not final:
                        pe.wait_ge(m["xe"], i + 2)
                    both(i, 2, bank[4], e_hT, MH, slice(0, HALF))
                    both(i, 2, bank[5], e_hT, MH, slice(HALF, D)).then_inc(m["used"], 1)

                gather(0)
                pe.wait_ge(m["fullest"], 1)
                pe.transpose(bank[2][0:1, 0:P], fullest, ident).then_inc(m["fullest_row"], 1)
                pair(0, first=True)
                pair(1, second=True)
                pe.wait_ge(m["rounds"], 1)
                n = pe.value_load(rounds[0:1, l, 0:1], min_val=PAIRS, max_val=PAIRS * PASSES)
                last = pe.value_load(rounds[0:1, l, 1:2], min_val=PAIRS - 1, max_val=PAIRS * PASSES - 1)
                with pe.Fori(2, last) as i:
                    pair(i)
                pair(last, final=True)
                turn_weights(n)
                combine(n, last=True)

            turn_normed(1)
            experts(0)

            turn_normed(2)
            for u in range(C_IN):
                pe.wait_ge(c_landed[u], 16)
                if u == 2:
                    pe.wait_ge(cc["biased"], 1)
                project(bank[2 * (u % 2):2 * (u % 2) + 2], slot_in(u)).then_inc(cc["used"], 1)
            pe.wait_ge(cc["roped"], 1)
            for c in range(4):
                for b in range(NB):
                    op = turn(bank[6 + c // 2][:, (c % 2) * S + b * P:(c % 2) * S + (b + 1) * P],
                              c_k[:, b, c * P:(c + 1) * P])
            op.then_inc(cc["k_turned"], 1)

            def turn_q(j, banks):
                pe.wait_ge(cc["roped"], j + 2)
                for c in range(4):
                    for b in range(NB):
                        lo = (c % 2) * S + b * P
                        op = turn(bank[banks[c // 2]][:, lo:lo + P],
                                  c_q[:, b, j * HALF + c * P:j * HALF + (c + 1) * P])
                op.then_inc(cc["q_turned"], 1)

            turn_q(0, (4, 5))

            def swa_scores(t):
                if t < 2:
                    pe.wait_ge(cc["k"], 1)
                    pe.wait_ge(cc["q"], 1)
                else:
                    pe.wait_ge(cc["masked"], t - 1)
                if t == SWA_HEADS // 2:
                    pe.wait_ge(cc["q"], 2)
                qT, kT = head_rows(c_qT, t), head_rows(c_kT, t, t // 4)
                dst = bank[4 + t % 2]
                pe.matmul(dst[:, 0:P], qT[:, 0:P], kT[:, 0:P], start=True, stop=True)
                pe.matmul(dst[:, P:TRI], qT[:, P:S], kT, start=True, stop=True).then_inc(cc["scores"], 1)

            def turn_p(t):
                pe.wait_ge(cc["prob"], t + 1)
                if t >= 2:
                    pe.wait_ge(cc["pT"], t - 1)
                for j in range(3):
                    op = turn(of_block(bank[6 + t % 2], j), c_p[:, t % 2, j * P:(j + 1) * P])
                op.then_inc(cc["p_turned"], 1)

            def swa_values(t):
                g = t // 4
                pe.wait_ge(cc["pT"], t + 1)
                if t == 0:
                    pe.wait_ge(cc["biased"], 3)
                if t % 4 == 0 and g >= 2:
                    pe.wait_ge(cc["o_norm"], g - 1)
                pT, dst, cols = c_pT[:, t % 2, :], bank[g % 2], slice(g * HD, (g + 1) * HD)
                lo, hi = (dst[:, b * S + (t % 4) * HD:b * S + (t % 4 + 1) * HD] for b in range(NB))
                pe.matmul(lo, pT[:, 0:P], c_v[:, 0, cols], start=True, stop=True)
                pe.matmul(hi, pT[:, P:S], c_v[:, 0, cols], start=True, stop=False)
                pe.matmul(hi, pT[:, S:TRI], c_v[:, 1, cols], start=False, stop=True).then_inc(cc["o"], 1)

            for t in range(SWA_HEADS + 3):
                if t < SWA_HEADS:
                    swa_scores(t)
                if 2 <= t < SWA_HEADS + 2:
                    turn_p(t - 2)
                if t >= 3:
                    swa_values(t - 3)
                if t == 3:
                    turn_q(1, (2, 3))
            pe.wait_ge(cc["o_norm"], 4)
            for b in range(NB):
                for c in range(KD):
                    op = turn(of_block(bank[2 + 2 * b + c // 4], c % 4), c_o[:, b, c * P:(c + 1) * P])
                    if c % 4 == 3:
                        op.then_inc(cc["o_turned"], 1)
            for part in range(2):
                pe.wait_ge(c_landed[C_IN + part], 16)
                if part == 0:
                    pe.wait_ge(cc["att_dve"], 2)
                else:
                    pe.wait_ge(cc["att_act"], 2)
                for b in range(NB):
                    for half in range(2):
                        for c in range(4 * part, 4 * part + 4):
                            op = out_proj(attT, c, b, half, slot_out(C_IN + part))
                    if part and b == 0:
                        op.then_inc(cc["out"], 1)
                op.then_inc(cc["used"], 1)
            turn_normed(3)
            experts(1)

        @block.vector
        def _(dve):
            steps = [0]

            def link(op):
                steps[0] += 1
                op.then_inc(dve_step, 1)
                dve.wait_ge(dve_step, steps[0])

            def norm(n):
                for b in range(NB):
                    dve.wait_ge(rooted, NB * n + b + 1)
                    if n < 2 * DEPTH:
                        dve.tensor_scalar(hr[:, b].rearrange("p k c -> p c k"),
                                          h[:, b, :].rearrange("p (c k) -> p c k", k=KD), rstd[:, n, b:b + 1], None,
                                          ALU.mult).then_inc(rms_done, 1)
                    else:
                        dve.scalar_tensor_tensor(out=flat(hr[:, b]), in0=h[:, b, :], scalar=rstd[:, n, b:b + 1],
                                                 in1=final_gain, op0=ALU.mult, op1=ALU.mult).then_inc(out_ready, 1)

            def spread_normed(n):
                dve.wait_ge(small_in, 160)
                for b in range(NB):
                    for q in range(2):
                        dve.wait_ge(turned, 4 * n + 2 * b + q + 1)
                        dve.tensor_tensor(hnT[:, 4 * q:4 * q + 4, b * P:(b + 1) * P],
                                          bank[4 + 2 * b + q][:].rearrange("p (k c) -> p k c", k=4),
                                          spread(gains[:, n, 4 * q:4 * q + 4], P), ALU.mult).then_inc(normed, 1)

            norm(0)
            spread_normed(0)

            def softplus(g):
                for s in range(2):
                    t = sb_w[:, 2 * (g % 2) + s, :]
                    dve.wait_ge(ab["log1p"], 2 * g + s + 1)
                    link(dve.scalar_tensor_tensor(out=t, in0=bank[4 + 2 * (g % 2) + s][:, 0:TRI], scalar=0.0, in1=t,
                                                  op0=ALU.max, op1=ALU.add))
                    dve.tensor_tensor(diagonal(t), diagonal(t), before2, ALU.mult).then_inc(ab["softplus"], 1)

            def causal_weights(g):
                for s in range(2):
                    t = sb_w[:, 2 * (g % 2) + s, :]
                    dve.wait_ge(ab["expw"], 2 * g + s + 1)
                    dve.scalar_tensor_tensor(out=diagonal(t), in0=diagonal(t), scalar=3e38, in1=before2, op0=ALU.min,
                                             op1=ALU.mult).then_inc(ab["weights"], 1)

            def concat(g):
                dve.wait_ge(ab["av"], g + 1)
                for b in range(NB):
                    op = dve.tensor_copy(catT[:, g, b * P:(b + 1) * P], bank[4 + 2 * (g % 2) + b][:, TRI:HALF])
                op.then_inc(ab["cat"], 1)

            def rotate(v):
                dve.wait_ge(ab["used"], 4 + v)
                if v:
                    dve.wait_ge(ab["roped"], v)
                for b in range(NB):
                    src = bank[2 * ((3 + v) % 2) + b][:]
                    dve.tensor_tensor(per_head(rope_a[:, b, :], 8), per_head(src, 8), over_heads(cos[:, b, :], 8), ALU.mult)
                    op = dve.tensor_tensor(per_head(rope_b[:, b, :], 8), swapped(src, 8), over_heads(sin[:, b, :], 8),
                                           ALU.mult)
                op.then_inc(ab["rope_mul"], 1)

            softplus(0)
            rotate(0)
            causal_weights(0)
            softplus(1)
            rotate(1)
            concat(0)
            causal_weights(1)
            softplus(2)
            concat(1)
            causal_weights(2)
            softplus(3)
            concat(2)
            causal_weights(3)
            dve.wait_ge(ab["rq_turned"], 1)
            for j in range(2):
                op = dve.tensor_copy(flat(r_qT[:, 2 * j:2 * j + 2, :]), bank[2 + j][:])
            op.then_inc(ab["rq"], 1)
            concat(3)
            dve.wait_ge(late_in, 32)
            for head in range(RET_HEADS):
                dve.wait_ge(ab["inner"], head + 1)
                if head >= 2:
                    dve.wait_ge(ab["ret_o"], head - 1)
                dve.tensor_tensor(r_w[:, head % 2, 0:S], bank[2 + head % 2][:, 0:S], decay[:, head, :], ALU.mult)
                dve.tensor_tensor(r_w[:, head % 2, S:TRI], bank[2 + head % 2][:, S:TRI], decay[:, head, 0:P],
                                  ALU.mult).then_inc(ab["decayed"], 1)
            dve.wait_ge(ab["ret_o"], RET_HEADS)
            by_head = [bank[4 + b][:].rearrange("p (h e) -> p h e", e=HD) for b in range(NB)]
            heads_of = [t.rearrange("p b (h e) -> p (b h) e", e=HD) for t in (r_c, r_sq)]
            sums = gn_sum.rearrange("p b h -> p (b h)")
            rs = gn_rstd.rearrange("p b h -> p (b h)")
            dve.tensor_reduce(gn_sum[:, 0], by_head[0], AX_X, ALU.add)
            link(dve.tensor_reduce(gn_sum[:, 1], by_head[1], AX_X, ALU.add))
            for b in range(NB):
                op = dve.scalar_tensor_tensor(out=r_c[:, b].rearrange("p (h e) -> p h e", e=HD), in0=spread(gn_sum[:, b], HD),
                                              scalar=-1.0 / HD, in1=by_head[b], op0=ALU.mult, op1=ALU.add)
            link(op)
            link(dve.tensor_tensor(flat(r_sq), flat(r_c), flat(r_c), ALU.mult))
            dve.tensor_reduce(sums, heads_of[1], AX_X, ALU.add).then_inc(ab["gn_var"], 1)
            dve.wait_ge(ab["gn_root"], 1)
            link(dve.scalar_tensor_tensor(out=heads_of[0], in0=heads_of[0], scalar=HD ** 0.5, in1=spread(rs, HD),
                                          op0=ALU.mult, op1=ALU.mult))
            dve.wait_ge(ab["act_evac"], 5)
            dve.tensor_tensor(flat(r_c), flat(r_c), flat(r_gate), ALU.mult).then_inc(ab["gn"], 1)
            dve.wait_ge(ab["gn_turned"], 1)
            for b in range(NB):
                op = dve.tensor_tensor(catT[:, 4:8, b * P:(b + 1) * P], bank[2 + b][:].rearrange("p (c n) -> p c n", c=4),
                                       spread(gn_gain[:], P), ALU.mult)
            op.then_inc(ab["gn_cat"], 1)

            def residual(b, banks):
                for half in range(2):
                    cols = slice(half * HALF, (half + 1) * HALF)
                    op = dve.tensor_tensor(h[:, b, cols], h[:, b, cols], bank[banks[2 * b + half]][:], ALU.add)
                op.then_inc(h_done, 1)

            dve.wait_ge(ab["out"], 1)
            residual(0, OUT_BANKS)
            dve.wait_ge(ab["used"], AB_UNITS)
            residual(1, OUT_BANKS)

            def experts(l):
                m = moe[l]
                dve.wait_ge(m["logits"], 1)
                link(dve.tensor_copy(logits, bank[0][:, 0:NB * CAP].rearrange("p (b n) -> p b n", b=NB)[:, :, 0:ROUTER]))
                link(dve.tensor_reduce(g_max, logits[:, :, 0:GROUPS], AX_X, ALU.max))
                dve.tensor_tensor(g_less, logits[:, :, 0:GROUPS], spread(g_max, GROUPS), ALU.subtract).then_inc(m["group_less"], 1)
                dve.wait_ge(m["group_less"], 1)
                link(dve.scalar_tensor_tensor(out=g_score, in0=g_less, scalar=0.0,
                                              in1=first4.unsqueeze(1).broadcast_to([P, NB, GROUPS]),
                                              op0=ALU.is_ge, op1=ALU.mult))
                link(dve.tensor_reduce(g_best, g_score, AX_X, ALU.max))
                link(dve.tensor_tensor(g_hot, g_score, spread(g_best, GROUPS), ALU.is_equal))
                link(dve.tensor_tensor(e_all, logits[:, :, GROUPS:ROUTER].rearrange("p b (g e) -> p b g e", g=GROUPS),
                                       spread(g_hot, PER_GROUP), ALU.mult))
                link(dve.tensor_reduce(e_log, e_all.rearrange("p b g e -> p b e g"), AX_X, ALU.add))
                link(dve.tensor_reduce(e_max, e_log, AX_X, ALU.max))
                link(dve.tensor_tensor(e_less, e_log, spread(e_max, PER_GROUP), ALU.subtract))
                firsts = first8.unsqueeze(1).broadcast_to([P, NB, PER_GROUP])
                link(dve.scalar_tensor_tensor(out=e_score, in0=e_less, scalar=0.0, in1=firsts, op0=ALU.is_ge, op1=ALU.mult))
                link(dve.tensor_reduce(e_best, e_score, AX_X, ALU.max))
                link(dve.tensor_tensor(e_hot1, e_score, spread(e_best, PER_GROUP), ALU.is_equal))
                link(dve.scalar_tensor_tensor(out=e_rest, in0=e_hot1, scalar=-BIG, in1=e_less, op0=ALU.mult, op1=ALU.add))
                dve.tensor_reduce(e_max2, e_rest, AX_X, ALU.max).then_inc(m["second"], 1)
                dve.wait_ge(m["second"], 1)
                link(dve.tensor_tensor(e_less, e_rest, spread(e_max2, PER_GROUP), ALU.subtract))
                link(dve.scalar_tensor_tensor(out=e_score, in0=e_less, scalar=0.0, in1=firsts, op0=ALU.is_ge, op1=ALU.mult))
                link(dve.tensor_reduce(e_best, e_score, AX_X, ALU.max))
                link(dve.tensor_tensor(e_hot2, e_score, spread(e_best, PER_GROUP), ALU.is_equal))
                link(dve.tensor_tensor(e_both, e_hot1, e_hot2, ALU.add))

                def by_group(t):
                    return t.unsqueeze(2).broadcast_to([P, NB, GROUPS, PER_GROUP])

                dve.tensor_tensor(chosen, by_group(e_both), spread(g_hot, PER_GROUP), ALU.mult).then_inc(m["chosen"], 1)
                dve.wait_ge(m["group_exp"], 1)
                link(dve.tensor_reduce(g_sum, g_exp, AX_X, ALU.add))
                dve.wait_ge(m["second_exp"], 1)
                link(dve.tensor_scalar(e_den, e_ratio, 1.0, None, ALU.add))
                link(dve.tensor_tensor(e_den, e_den, g_sum, ALU.mult))
                link(dve.reciprocal(gate1, e_den))
                link(dve.tensor_tensor(gate2, gate1, e_ratio, ALU.mult))
                link(dve.tensor_tensor(e_gate1, e_hot1, spread(gate1, PER_GROUP), ALU.mult))
                link(dve.tensor_tensor(e_gate2, e_hot2, spread(gate2, PER_GROUP), ALU.mult))
                link(dve.tensor_tensor(e_gates, e_gate1, e_gate2, ALU.add))
                link(dve.tensor_tensor(gates, by_group(e_gates), spread(g_hot, PER_GROUP), ALU.mult))
                dve.wait_ge(m["ranked"], 1)
                rows = rank.rearrange("p b g e -> p b (g e)")
                link(dve.scalar_tensor_tensor(out=rank.rearrange("p b g e -> p (b g e)"), in0=bank[1][:, 0:NB * EXPERTS],
                                              scalar=1.0, in1=chosen.rearrange("p b g e -> p (b g e)"),
                                              op0=ALU.add, op1=ALU.mult))
                for j in range(PASSES):
                    cols = slice(j * EXPERTS, (j + 1) * EXPERTS)
                    dve.tensor_copy(gate_all[:, :, cols], gates.rearrange("p b g e -> p b (g e)"))
                    op = dve.tensor_scalar(rank_all[:, :, cols], rows, -1.0 - CAP * j, None, ALU.add)
                link(op)

                def one_hot(i, first=False):
                    if not first:
                        dve.wait_ge(m["pick_w"], i)
                    dve.tensor_tensor(pair_rows(pick), slots.unsqueeze(1).unsqueeze(1).broadcast_to([P, NB, 2, CAP]),
                                      of_pair(rank_all, i), ALU.is_equal).then_inc(m["pick"], 1)

                one_hot(0, first=True)
                dve.tensor_reduce(fullest, rank.rearrange("p b g e -> p (b g e)"), AX_X, ALU.max).then_inc(m["fullest"], 1)

                def take_rows(i):
                    dve.wait_ge(m["gathered"], i + 1)
                    for q in range(2):
                        op = dve.tensor_tensor(xeT[:, 4 * q:4 * q + 4, :], bank[4 + q][:].rearrange("p (k c) -> p k c", k=4),
                                               spread(gains[:, 2 * l + 1, 4 * q:4 * q + 4], P), ALU.mult)
                    op.then_inc(m["xe"], 1)

                def hidden(i):
                    dve.wait_ge(m["silu"], i + 1)
                    dve.wait_ge(m["used"], 3 * i + 2)
                    dve.tensor_tensor(e_h, e_silu, bank[7][:], ALU.mult).then_inc(m["hidden"], 1)

                def copy_low(i):
                    dve.wait_ge(m["used"], 3 * i)
                    dve.tensor_copy(e_y[:, 0:HALF], bank[4][:]).then_inc(m["y_low"], 1)

                take_rows(0)
                dve.wait_ge(m["fullest_row"], 1)
                link(dve.tensor_reduce(fullest_all[0:1], bank[2][0:1, 0:P], AX_X, ALU.max))
                for j in range(1, PASSES):
                    op = dve.tensor_scalar(more[0:1, j - 1:j], fullest_all[0:1], CAP * j + 0.5, float(PAIRS),
                                           ALU.is_ge, ALU.mult)
                link(op)
                link(dve.tensor_reduce(fullest_all[0:1], more[0:1], AX_X, ALU.add))
                dve.tensor_scalar(rounds[0:1, l, 0:1], fullest_all[0:1], float(PAIRS), None, ALU.add)
                dve.tensor_scalar(rounds[0:1, l, 1:2], fullest_all[0:1], float(PAIRS - 1), None,
                                  ALU.add).then_inc(m["rounds"], 1)
                one_hot(1)
                hidden(0)
                take_rows(1)
                dve.wait_ge(m["rounds"], 1)
                n = dve.value_load(rounds[0:1, l, 0:1], min_val=PAIRS, max_val=PAIRS * PASSES)
                last = dve.value_load(rounds[0:1, l, 1:2], min_val=PAIRS - 1, max_val=PAIRS * PASSES - 1)
                with dve.Fori(1, last) as i:
                    copy_low(i)
                    one_hot(i + 1)
                    hidden(i)
                    take_rows(i + 1)
                copy_low(last)
                hidden(last)
                copy_low(n)
                dve.wait_ge(m["combined"], 1)
                for b in range(NB):
                    residual(b, [0, 1, 2, 3])

            norm(1)
            spread_normed(1)
            dve.wait_ge(late_in, 32)
            experts(0)

            norm(2)
            spread_normed(2)
            dve.wait_ge(bias_in, 48)
            link(dve.tensor_scalar(sink_neg[:], sinks_b[:], -1.0, None, ALU.mult))
            for u in range(C_IN):
                heads = SB_HEADS if u else KV_HEADS
                w = heads * HD
                dve.wait_ge(cc["used"], u + 1)
                for b in range(NB):
                    op = dve.tensor_tensor(c_in[:, b, :], bank[2 * (u % 2) + b][:], c_bin[:, C_COLS[u]:C_COLS[u] + HALF],
                                           ALU.add)
                op.then_inc(cc["biased"], 1)
                dve.wait_ge(cc["biased"], u + 1)
                if u == 0:
                    dve.tensor_copy(c_v, c_in[:, :, w:2 * w])
                for b in range(NB):
                    op = dve.tensor_tensor(per_head(c_a[:, b, 0:w], heads), per_head(c_in[:, b, 0:w], heads),
                                           over_heads(cos[:, b, :], heads), ALU.mult)
                link(op)
                dve.wait_ge(cc["rope_swap"], u + 1)
                if u:
                    op = dve.tensor_tensor(c_q[:, :, (u - 1) * HALF:u * HALF], c_a, c_b, ALU.add)
                else:
                    for copy in range(2):
                        for b in range(NB):
                            op = dve.tensor_tensor(
                                c_k[:, b].rearrange("p (h a c) -> p h a c", h=KV_HEADS, a=2)[:, :, copy, :],
                                c_a[:, b, 0:w].rearrange("p (h c) -> p h c", c=HD),
                                c_b[:, b, 0:w].rearrange("p (h c) -> p h c", c=HD), ALU.add)
                op.then_inc(cc["roped"], 1)

            def masked(t):
                dve.wait_ge(cc["scores"], t + 1)
                if t >= 2:
                    dve.wait_ge(cc["prob"], t - 1)
                for b, cols in enumerate((slice(0, P), slice(P, TRI))):
                    op = dve.tensor_tensor_reduce(out=c_s[:, t % 2, cols], in0=bank[4 + t % 2][:, cols],
                                                  in1=swa_mask[:, cols], scale=1.0, scalar=sink_neg[:, t:t + 1],
                                                  op0=ALU.add, op1=ALU.min, accum_out=c_min[:, t, b:b + 1])
                op.then_inc(cc["masked"], 1)
                if t % 4 == 3:
                    dve.wait_ge(cc["masked"], t + 1)
                    dve.tensor_tensor(c_den[:, t - 3:t + 1, :], c_min[:, t - 3:t + 1, :],
                                      spread(sink_neg[:, t - 3:t + 1], NB), ALU.subtract).then_inc(cc["sink"], 1)

            def copy_p(t):
                dve.wait_ge(cc["p_turned"], t + 1)
                if t >= 2:
                    dve.wait_ge(cc["o"], t - 1)
                dve.tensor_copy(c_pT[:, t % 2, :], bank[6 + t % 2][:, 0:TRI]).then_inc(cc["pT"], 1)

            def normalise(g):
                hs = slice(4 * g, 4 * g + 4)
                dve.wait_ge(cc["prob"], 4 * g + 4)
                dve.wait_ge(cc["sink_exp"], g + 1)
                link(dve.tensor_tensor(c_den[:, hs, :], c_den[:, hs, :], c_sum[:, hs, :], ALU.add))
                link(dve.reciprocal(c_den[:, hs, :], c_den[:, hs, :]))
                dve.wait_ge(cc["o"], 4 * g + 4)
                for b in range(NB):
                    op = dve.tensor_tensor(c_o[:, b, g * S:(g + 1) * S].rearrange("p (h e) -> p h e", e=HD),
                                           bank[g % 2][:, b * S:(b + 1) * S].rearrange("p (h e) -> p h e", e=HD),
                                           spread(c_den[:, hs, b], HD), ALU.mult)
                op.then_inc(cc["o_norm"], 1)

            for t in range(SWA_HEADS + 3):
                if t < SWA_HEADS:
                    masked(t)
                if 2 <= t < SWA_HEADS + 2:
                    copy_p(t - 2)
                if t >= 7 and t % 4 == 3:
                    normalise((t - 7) // 4)
            normalise(3)
            for b in range(NB):
                dve.wait_ge(cc["o_turned"], 2 * b + 1)
                dve.tensor_copy(attT[:, 0:4, b * P:(b + 1) * P],
                                bank[2 + 2 * b][:].rearrange("p (c n) -> p c n", c=4)).then_inc(cc["att_dve"], 1)
            dve.wait_ge(cc["bias_h"], 1)
            dve.wait_ge(cc["out"], 1)
            residual(0, OUT_BANKS)
            dve.wait_ge(cc["used"], C_UNITS)
            residual(1, OUT_BANKS)
            norm(3)
            spread_normed(3)
            experts(1)
            norm(4)


_INS = ["x", "attn_norm_g", "ffn_norm_g", "w_in_ab", "w_out_ab", "ret_gn_g", "w_in_c", "b_in_c", "sinks",
        "w_out_c", "b_out_c", "w_group", "w_expert_router", "w_gate", "w_up", "w_down", "final_norm_g"]


def kernel(**inputs):
    import concourse.bacc as bacc
    from concourse.bass_utils import run_bass_kernel_spmd

    nc = bacc.Bacc("TRN2", target_bir_lowering=False, num_devices=1)
    arrays = {f"in_{name}": np.ascontiguousarray(inputs[name]) for name in _INS}
    arrays["early_table"], arrays["late_table"] = constant_tables()
    args = [nc.dram_tensor(name, a.shape, F32, kind="ExternalInput").ap() for name, a in arrays.items()]
    args.append(nc.dram_tensor("out", (1, S, D), F32, kind="ExternalOutput").ap())
    hybrid_trunk(nc, *args)
    return run_bass_kernel_spmd(nc, [arrays], core_ids=[0]).results[0]["out"]
```

```python
from contextlib import ExitStack

import numpy as np

import concourse.bass as bass
from concourse import mybir

F32 = mybir.dt.float32
I32 = mybir.dt.int32
ALU = mybir.AluOpType
ACT = mybir.ActivationFunctionType
AX_X = mybir.AxisListType.X

P = 128
D = 1024
S = 256
NB = S // P
KD = D // P
HD = 64
HALF = 512
DEPTH = 2

SB_HEADS = 8
SB_GROUPS = SB_HEADS // 2
RET_HEADS = 8
TRI = 384
AB_IN = 7
AB_UNITS = AB_IN + 2

SWA_HEADS = 16
KV_HEADS = 4
C_IN = 3
C_UNITS = C_IN + 2

EXPERTS = 32
GROUPS = 4
PER_GROUP = EXPERTS // GROUPS
DE = 512
MH = DE // P
CAP = 64
PASSES = S // CAP
PAIRS = EXPERTS // 2
ROUTER = GROUPS + EXPERTS

RING = 6
UNIT = 4096
PARKED = 3
ARENA = 16800
EPS = 1e-6
BIG = 1e30

EARLY = {"gains": 2 * DEPTH * KD, "ident": 128, "before": 128, "neg_from": 128, "cos": NB * HD, "sin": NB * HD}
LATE = {"router": DEPTH * KD * ROUTER, "gn_gain": 4, "swa_mask": TRI, "slots": CAP, "first4": GROUPS,
        "first8": PER_GROUP}


def tables(attn_norm_g, ffn_norm_g, ret_gn_g, w_group, w_expert_router):
    f32 = np.float32
    p, c = np.arange(P)[:, None], np.arange(P)[None, :]
    before = (p < c).astype(f32)
    inv = f32(10000.0) ** (-np.arange(0, HD, 2, dtype=f32) / f32(HD))
    ang = np.arange(S, dtype=f32)[:, None] * inv[None, :]
    cos, sin = np.cos(ang), np.sin(ang)
    cos2 = np.concatenate([cos, cos], 1).reshape(NB, P, HD).transpose(1, 0, 2).reshape(P, -1)
    sin2 = np.concatenate([-sin, sin], 1).reshape(NB, P, HD).transpose(1, 0, 2).reshape(P, -1)
    gains = np.stack([attn_norm_g, ffn_norm_g], 1).reshape(2 * DEPTH, P, KD).transpose(1, 0, 2).reshape(P, -1)
    early = np.concatenate([gains, np.eye(P, dtype=f32), before, before - 1, cos2, sin2], 1)
    log_g = np.log(f32(1.0) - f32(2.0) ** (f32(-5.0) - np.arange(RET_HEADS, dtype=f32)))
    ahead = np.arange(S, dtype=f32)[None, None, :] - np.arange(P, dtype=f32)[:, None, None]
    decay = np.where(ahead >= 0, np.exp(log_g[None, :, None] * np.maximum(ahead, 0)), 0) * HD ** -0.5
    decay = np.concatenate([decay, decay[:, :, 0:P]], 2)
    diag = np.where(c <= p, 0, BIG)
    swa = np.concatenate([diag, np.where(c > p, 0, BIG), diag], 1)
    row = np.concatenate([np.arange(CAP), np.arange(GROUPS, 0, -1), np.arange(PER_GROUP, 0, -1)])
    router = np.concatenate([w_group, w_expert_router], 2).reshape(DEPTH, P, KD, ROUTER)
    router = router.transpose(1, 0, 2, 3).reshape(P, -1)
    gn_gain = ret_gn_g[0].reshape(4, P).T
    late = np.concatenate([router, gn_gain, swa, np.tile(row, (P, 1))], 1)
    return early.astype(f32), late.astype(f32), decay.reshape(P, -1).astype(f32)


def hybrid_trunk(nc, x, w_in_ab, w_out_ab, w_in_c, b_in_c, sinks, w_out_c, b_out_c, w_gate, w_up, w_down,
                 final_norm_g, early_table, late_table, decay_table, out):
    ctx = ExitStack()
    with ctx:
        ctx.enter_context(nc.allow_non_contiguous_dma(reason="rows of sinks and biases for every partition"))

        def sb(name, shape, dt=F32):
            return ctx.enter_context(nc.sbuf_tensor(name, shape, dt))

        def sem(name):
            return ctx.enter_context(nc.semaphore(name))

        ring = sb("ring", [P, RING, UNIT])
        h = sb("h", [P, NB, D])
        hr = sb("hr", [P, NB, KD, P])
        hnT = sb("hnT", [P, KD, S])
        early = sb("early", [P, sum(EARLY.values())])
        late = sb("late", [P, sum(LATE.values())])
        ones = sb("ones", [P, P])
        neg_ones = sb("neg_ones", [P, P])
        minus_half = sb("minus_half", [P, NB * RET_HEADS])
        sinks_b = sb("sinks_b", [P, SWA_HEADS])
        sink_neg = sb("sink_neg", [P, SWA_HEADS])
        ms = sb("ms", [P, 2 * DEPTH + 1, NB])
        rstd = sb("rstd", [P, 2 * DEPTH + 1, NB])
        rank_all = sb("rank_all", [P, NB, PASSES * EXPERTS])
        gate_all = sb("gate_all", [P, NB, PASSES * EXPERTS])
        tmp = sb("tmp", [P, 1080])
        rounds = sb("rounds", [1, DEPTH, 4], I32)
        arena = sb("arena", [P, ARENA])

        pos = [0]

        def carve(*shape, at=None):
            n = int(np.prod(shape))
            lo = pos[0] if at is None else at
            if at is None:
                pos[0] += n
            assert lo + n <= ARENA
            v = arena[:, lo:lo + n]
            if len(shape) == 2:
                v = v.rearrange("p (a b) -> p a b", a=shape[0])
            if len(shape) == 3:
                v = v.rearrange("p (a b c) -> p a b c", a=shape[0], b=shape[1])
            return v

        catT, r_gate, rope_a = carve(KD, S), carve(NB, HALF), carve(NB, HALF)
        assert pos[0] <= ARENA - PARKED * UNIT
        sb_qT, sb_kT, sb_v = carve(SB_GROUPS, S), carve(SB_GROUPS, S), carve(NB, HALF)
        sb_w = carve(4, TRI)
        r_q, r_k, r_v, rope_b = (carve(NB, HALF) for _ in range(4))
        r_w = carve(2, TRI)
        decay = carve(RET_HEADS, TRI)
        r_qT, r_kT = sb_qT, sb_kT
        r_c, r_sq = rope_a, rope_b
        r_oT = r_sq.rearrange("p b c -> p (b c)").rearrange("p (c n) -> p c n", c=4)
        pos[0] = 0
        c_q, c_o = carve(NB, D), carve(NB, D)
        attT = carve(KD, S, at=0)
        assert pos[0] <= ARENA - PARKED * UNIT
        c_k, c_v = carve(NB, KV_HEADS * 2 * HD), carve(NB, KV_HEADS * HD)
        c_in, c_a, c_b = carve(NB, HALF), carve(NB, HALF), carve(NB, HALF)
        c_kT = carve(KV_HEADS, S)
        c_s, c_p, c_pT = carve(2, TRI), carve(2, TRI), carve(2, TRI)
        c_qT = [carve(4, S), hnT[:, 0:4, :]]
        c_min, c_sum, c_den = (carve(SWA_HEADS, NB) for _ in range(3))
        c_bin, c_bout = carve(C_IN * HALF), carve(D)
        pos[0] = 0
        pick, pick_w = carve(NB, P), carve(NB, P)
        xeT = carve(KD, P)
        e_silu, e_h, e_hT = carve(DE), carve(DE), carve(MH, P)
        e_y = carve(D)
        pick_wT = carve(S)
        parked = [carve(UNIT, at=ARENA - (PARKED - j) * UNIT) for j in range(PARKED)]
        final_gain = carve(D, at=ARENA - D)
        assert pos[0] <= ARENA - PARKED * UNIT

        spent = [0]

        def small(*shape):
            n = int(np.prod(shape))
            v = tmp[:, spent[0]:spent[0] + n]
            spent[0] += n
            if len(shape) == 2:
                v = v.rearrange("p (a b) -> p a b", a=shape[0])
            if len(shape) == 3:
                v = v.rearrange("p (a b c) -> p a b c", a=shape[0], b=shape[1])
            return v

        g_max, g_sum, g_best = (small(NB) for _ in range(3))
        g_less, g_exp, g_score, g_hot = (small(NB, GROUPS) for _ in range(4))
        e_max, e_best, e_max2, e_ratio, e_den, gate1, gate2 = (small(NB, GROUPS) for _ in range(7))
        e_less, e_score, e_hot1, e_rest, e_hot2, e_both, e_gate1, e_gate2, chosen, rank = (
            small(NB, GROUPS, PER_GROUP) for _ in range(10))
        fullest, fullest_all = small(1), small(1)
        more = small(PASSES - 1)
        logits_T = small(S)
        gn_sum, gn_rstd = small(NB, RET_HEADS), small(NB, RET_HEADS)

        spot = {}
        for table, parts in ((early, EARLY), (late, LATE)):
            lo = 0
            for name, n in parts.items():
                spot[name] = table[:, lo:lo + n]
                lo += n
        gains = spot["gains"].rearrange("p (n k) -> p n k", k=KD)
        ident, before, neg_from = spot["ident"], spot["before"], spot["neg_from"]
        cos = spot["cos"].rearrange("p (b c) -> p b c", b=NB)
        sin = spot["sin"].rearrange("p (b c) -> p b c", b=NB)
        router = spot["router"].rearrange("p (l k n) -> p l k n", l=DEPTH, k=KD)
        gn_gain, swa_mask, slots = spot["gn_gain"], spot["swa_mask"], spot["slots"]
        first4, first8 = spot["first4"], spot["first8"]

        bank = [ctx.enter_context(nc.psum_tensor(f"bank{i}", [P, HALF], F32)) for i in range(8)]

        early_in, late_in = sem("early_in"), sem("late_in")
        x_in = [sem(f"x_in{b}") for b in range(NB)]
        decay_in = sem("decay_in")
        rows_in = [sem("bias_rows_in"), sem("final_gain_in")]
        ones_set = sem("ones_set")
        dve_step, act_step, pool_step = sem("dve_step"), sem("act_step"), sem("pool_step")
        squares = sem("squares")
        rooted = sem("rooted")
        rms_done = sem("rms_done")
        turned = sem("turned")
        normed = sem("normed")
        h_done = sem("h_done")
        out_ready = sem("out_ready")
        out_done = sem("out_done")
        ab = {n: sem("ab_" + n) for n in (
            "used", "act_evac", "rope_mul", "roped", "z", "log1p", "softplus", "cum", "expw",
            "weights", "av", "cat", "rq_turned", "rk_turned", "rq", "rk", "inner", "decayed", "ret_o", "oT", "ret_turned",
            "gn", "gn_var", "gn_root", "gn_turned", "gn_cat", "out")}
        ab_landed = [sem(f"ab_landed{i}") for i in range(RING)]
        cc = {n: sem("c_" + n) for n in (
            "used", "biased", "rope_swap", "roped", "k_turned", "k", "q_turned", "q", "scores", "masked",
            "prob", "sink", "sink_exp", "p_turned", "pT", "o", "o_norm", "low_turned", "att_low", "high_turned",
            "att_high_act", "att_high_dve",
            "out", "bias_h")}
        c_landed = [sem(f"c_landed{i}") for i in range(C_UNITS)]
        moe = []
        for l in range(DEPTH):
            m = {n: sem(f"m{l}_{n}") for n in (
                "logits_T", "logits_sb", "down_low", "logits", "gates", "group_less", "group_exp", "second", "second_exp", "chosen", "ranked", "fullest",
                "fullest_row", "rounds", "gathered", "xe", "silu", "hidden", "h_turned", "hT",
                "pickT", "pickT_sb", "y_low", "y_high", "pick", "pick_w", "used", "combined")}
            m["parked"] = [sem(f"m{l}_parked{i}") for i in range(PARKED)]
            m["landed"] = [sem(f"m{l}_landed{i}") for i in range(RING)]
            moe.append(m)

        x_v = x[0].rearrange("(b p) d -> p b d", p=P)
        out_v = out[0].rearrange("(b p) d -> p b d", p=P)
        w_ab_v = w_in_ab[0].rearrange("(p k) n -> p k n", k=KD)
        w_c_v = w_in_c[0].rearrange("(p k) n -> p k n", k=KD)
        wo_ab_v = w_out_ab[0].rearrange("(u c p) n -> u p c n", u=2, p=P)
        wo_c_v = w_out_c[0].rearrange("(u c p) n -> u p c n", u=2, p=P)
        C_COLS = [2 * HALF, 0, HALF]
        OUT_BANKS = [0, 1, 6, 7]
        C_OUT_BANKS = [2, 3, 6, 7]

        def as_in(t):
            return t.rearrange("p (k n) -> p k n", k=KD)

        def as_out(t):
            return t.rearrange("p (c n) -> p c n", c=4)

        def slot_in(s):
            return as_in(ring[:, s, :])

        def slot_out(s):
            return as_out(ring[:, s, :])

        def c_slot(u):
            return (AB_UNITS + u) % RING

        def moe_slot(l, j):
            return (AB_UNITS + l * C_UNITS + j) % RING

        def flat(v):
            return v.rearrange("p a b -> p (a b)")

        def row_bcast(v, n):
            return bass.AP(v.tensor, v.offset, [[0, P], [1, n]])

        def per_head(v, heads):
            return v.rearrange("p (h a c) -> p h a c", h=heads, a=2)

        def swapped(v, heads):
            ps, pn = v.ap[0]
            return bass.AP(v.tensor, v.offset + HD // 2, [[ps, pn], [HD, heads], [-HD // 2, 2], [1, HD // 2]])

        def over_heads(v, heads):
            ps, pn = v.ap[0]
            return bass.AP(v.tensor, v.offset, [[ps, pn], [0, heads], [HD // 2, 2], [1, HD // 2]])

        def spread(v, n):
            return v.unsqueeze(len(v.shape)).broadcast_to([*v.shape, n])

        def diagonal(v):
            return v.rearrange("p (a c) -> p a c", a=3)[:, 0:3:2, :]

        def of_block(t, b):
            return t[:, b * P:(b + 1) * P]

        def pair_rows(t):
            return t.rearrange("p b (s c) -> p b s c", s=2)

        def of_pair(t, i):
            return spread(t[:, :, bass.ds(2 * i, 2)], CAP)

        before2 = before.unsqueeze(1).broadcast_to([P, 2, P])

        def head_rows(t, head, chunk=None):
            off = (head % 2) * HD
            return t[off:off + HD, head // 2 if chunk is None else chunk, :]

        block = ctx.enter_context(nc.Block())

        @block.sync
        def _(sp):
            def expert_unit(l, e, kind):
                one = bass.ds(e, 1)
                if kind < 2:
                    return (w_gate, w_up)[kind][l, one].rearrange("a (p k) n -> p (a k) n", k=KD)
                return w_down[l, one].rearrange("a (m p) n -> p (a m) n", p=P)

            def load(l, i, j):
                sp.dma_start((slot_in if j < 4 else slot_out)(moe_slot(l, j)),
                             expert_unit(l, 2 * i + j % 2, j // 2)).then_inc(moe[l]["landed"][j], 16)

            def park(l, j):
                sp.dma_start((as_in if j < 4 else as_out)(parked[j]),
                             expert_unit(l, 2 + j % 2, j // 2)).then_inc(moe[l]["parked"][j], 16)

            def experts(l, slot_free, park_free, rows):
                m = moe[l]
                for j in range(4):
                    slot_free(j)
                    load(l, 0, j)
                park_free()
                park(l, 0)
                slot_free(4)
                load(l, 0, 4)
                for j in range(1, PARKED):
                    park(l, j)
                slot_free(5)
                load(l, 0, 5)
                sp.wait_ge(m["used"], 1)
                for j in range(2):
                    load(l, 2, j)
                sp.wait_ge(m["used"], 2)
                for j in range(PARKED, 4):
                    load(l, 1, j)
                for j in range(2, PARKED):
                    load(l, 2, j)
                sp.wait_ge(m["used"], 3)
                for j in range(4, RING):
                    load(l, 1, j)
                sp.wait_ge(m["used"], 4)
                for j in range(2):
                    sp.dma_start(as_in(parked[j]), expert_unit(l, 6 + j, 0)).then_inc(m["parked"][j], 16)
                sp.wait_ge(m["used"], 5)
                for j in range(PARKED, 4):
                    load(l, 2, j)
                sp.wait_ge(m["used"], 6)
                for j in range(4, RING):
                    load(l, 2, j)
                for dst, src, n in rows:
                    sp.dma_start(dst, row_bcast(src, n)).then_inc(rows_in[l], 16)
                sp.wait_ge(m["rounds"], 1)
                last = sp.value_load(rounds[0:1, l, 1:2], min_val=PAIRS - 1, max_val=PAIRS * PASSES - 1)
                before_last = sp.value_load(rounds[0:1, l, 2:3], min_val=PAIRS - 2, max_val=PAIRS * PASSES - 2)
                half = sp.value_load(rounds[0:1, l, 3:4], min_val=PAIRS // 2 - 1, max_val=PAIRS * PASSES // 2 - 1)

                def next_gates(i, odd):
                    for j in range(2):
                        e = ((i + 2) % PAIRS) * 2 + j
                        sp.compute_val(e * (D * DE) * 4)
                        sp.wait_ge(m["used"], 3 * i + 1)
                        sp.dma_start(as_in(parked[j]) if odd else slot_in(moe_slot(l, j)),
                                     expert_unit(l, e, 0)).then_inc(m["parked" if odd else "landed"][j], 16)

                def next_rest(i):
                    for j in range(2, RING):
                        e = ((i + 1) % PAIRS) * 2 + j % 2
                        sp.compute_val(e * (D * DE) * 4)
                        sp.wait_ge(m["used"], 3 * i + (j // 2 + 1))
                        sp.dma_start((slot_in if j < 4 else slot_out)(moe_slot(l, j)),
                                     expert_unit(l, e, j // 2)).then_inc(m["landed"][j], 16)

                with sp.Fori(1, half) as t:
                    for odd in range(2):
                        next_rest(2 * t + odd)
                        next_gates(2 * t + odd, odd)
                next_rest(before_last)
                return last

            for b in range(NB):
                sp.dma_start(h[:, b, :], x_v[:, b, :]).then_inc(x_in[b], 16)
            for u in range(AB_UNITS):
                s = u % RING
                if u >= RING:
                    sp.wait_ge(ab["used"], u - RING + 1)
                if u < AB_IN:
                    sp.dma_start(slot_in(s), w_ab_v[:, :, u * HALF:(u + 1) * HALF]).then_inc(ab_landed[s], 16)
                else:
                    sp.dma_start(slot_out(s), wo_ab_v[u - AB_IN]).then_inc(ab_landed[s], 16)

            def after_ab(j):
                sp.wait_ge(ab["used"], AB_UNITS - RING + j + 1)

            def after_c(j):
                if j == 0:
                    sp.wait_ge(moe[0]["used"], 3 * last + 3)
                else:
                    sp.wait_ge(cc["used"], j)

            def ab_tiles_free():
                sp.wait_ge(ab["gn_var"], 1)

            def c_tiles_free():
                sp.wait_ge(cc["o_norm"], 4)
                sp.wait_ge(cc["bias_h"], 1)

            last = experts(0, after_ab, ab_tiles_free,
                           [(sinks_b[:], sinks, SWA_HEADS), (c_bin, b_in_c, C_IN * HALF), (c_bout, b_out_c, D)])
            for u in range(C_UNITS):
                sp.wait_ge(moe[0]["used"], 3 * last + (u // 2 + 1) if u >= 2 else 3 * last)
                if u < C_IN:
                    sp.dma_start(slot_in(c_slot(u)), w_c_v[:, :, C_COLS[u]:C_COLS[u] + HALF]).then_inc(c_landed[u], 16)
                else:
                    sp.dma_start(slot_out(c_slot(u)), wo_c_v[u - C_IN]).then_inc(c_landed[u], 16)
            experts(1, after_c, c_tiles_free, [(final_gain, final_norm_g, D)])
            for b in range(NB):
                sp.wait_ge(out_ready, b + 1)
                sp.dma_start(out_v[:, b, :], hr[:, b].rearrange("p k c -> p (k c)")).then_inc(out_done, 16)
            sp.wait_ge(out_done, 16 * NB)

        @block.gpsimd
        def _(pool):
            steps = [0]

            def link(op):
                steps[0] += 1
                op.then_inc(pool_step, 1)
                pool.wait_ge(pool_step, steps[0])

            link(pool.memset(minus_half[:], -0.5))
            pool.memset(ones[:], 1.0).then_inc(ones_set, 1)
            pool.memset(neg_ones[:], -1.0).then_inc(ones_set, 1)

            def inverse_rms(n):
                for b in range(NB):
                    pool.wait_ge(squares, NB * n + b + 1)
                    link(pool.tensor_scalar(rstd[:, n, b:b + 1], ms[:, n, b:b + 1], EPS, None, ALU.add))
                    pool.tensor_tensor(rstd[:, n, b:b + 1], rstd[:, n, b:b + 1], minus_half[:, 0:1],
                                       ALU.pow).then_inc(rooted, 1)

            inverse_rms(0)
            for v, dst in enumerate((r_q, r_k)):
                pool.wait_ge(ab["rope_mul"], v + 1)
                pool.tensor_tensor(flat(dst), flat(rope_a), flat(rope_b), ALU.add).then_inc(ab["roped"], 1)

            def experts(l):
                m = moe[l]

                def weighted(i):
                    pool.tensor_tensor(pair_rows(pick_w), pair_rows(pick), of_pair(gate_all, i),
                                       ALU.mult).then_inc(m["pick_w"], 1)

                pool.wait_ge(m["gates"], 1)
                weighted(0)
                pool.wait_ge(m["rounds"], 1)
                n = pool.value_load(rounds[0:1, l, 0:1], min_val=PAIRS, max_val=PAIRS * PASSES)
                with pool.Fori(1, n) as i:
                    pool.wait_ge(m["pick"], i + 1)
                    pool.wait_ge(m["pickT"], i)
                    weighted(i)

            pool.wait_ge(ab["gn_var"], 1)
            link(pool.tensor_scalar(flat(gn_rstd), flat(gn_sum), HD * EPS, None, ALU.add))
            pool.tensor_tensor(flat(gn_rstd), flat(gn_rstd), minus_half[:], ALU.pow).then_inc(ab["gn_root"], 1)
            inverse_rms(1)
            experts(0)
            inverse_rms(2)
            for u in range(C_IN):
                heads = SB_HEADS if u else KV_HEADS
                pool.wait_ge(cc["biased"], u + 1)
                if u:
                    pool.wait_ge(cc["roped"], u)
                for b in range(NB):
                    op = pool.tensor_tensor(per_head(c_b[:, b, 0:heads * HD], heads),
                                            swapped(c_in[:, b, 0:heads * HD], heads),
                                            over_heads(sin[:, b, :], heads), ALU.mult)
                op.then_inc(cc["rope_swap"], 1)
            pool.wait_ge(rows_in[0], 48)
            for b in range(NB):
                op = pool.tensor_tensor(h[:, b, :], h[:, b, :], c_bout, ALU.add)
            op.then_inc(cc["bias_h"], 1)
            inverse_rms(3)
            experts(1)
            inverse_rms(4)

        @block.scalar
        def _(act):
            steps = [0]

            def link(op):
                steps[0] += 1
                op.then_inc(act_step, 1)
                act.wait_ge(act_step, steps[0])

            act.dma_start(early[:], early_table).then_inc(early_in, 16)
            def mean_squares(n):
                for b in range(NB):
                    if n == 0:
                        act.wait_ge(x_in[b], 16)
                    else:
                        act.wait_ge(h_done, NB * (n - 1) + b + 1)
                    act.activation(flat(hr[:, b]), h[:, b, :], ACT.Square, scale=D ** -0.5,
                                   accum_out=ms[:, n, b:b + 1]).then_inc(squares, 1)

            mean_squares(0)
            act.dma_start(late[:], late_table).then_inc(late_in, 16)
            act.dma_start(flat(decay), decay_table).then_inc(decay_in, 16)

            def evac(u, dst, func, scale):
                act.wait_ge(ab["used"], u + 1)
                for j in range(2):
                    op = act.activation(dst[j], bank[2 * (u % 2) + j][:], func, scale=scale)
                op.then_inc(ab["act_evac"], 1)

            def chunks(t):
                return [flat(t[:, 2 * j:2 * j + 2, :]) for j in range(2)]

            def blocks(t):
                return [t[:, b, :] for b in range(NB)]

            def log1p(g):
                act.wait_ge(ab["z"], g + 1)
                for s in range(2):
                    t = sb_w[:, 2 * (g % 2) + s, :]
                    link(act.activation(t, bank[4 + 2 * (g % 2) + s][:, 0:TRI], ACT.Abs))
                    link(act.activation(t, t, ACT.Exp, scale=-1.0))
                    act.activation(t, t, ACT.Ln, bias=1.0).then_inc(ab["log1p"], 1)

            def stick_weights(g):
                act.wait_ge(ab["cum"], g + 1)
                for s in range(2):
                    act.activation(sb_w[:, 2 * (g % 2) + s, :], bank[4 + 2 * (g % 2) + s][:, 0:TRI],
                                   ACT.Exp).then_inc(ab["expw"], 1)

            evac(0, chunks(sb_qT), ACT.Copy, HD ** -0.5)
            evac(1, chunks(sb_kT), ACT.Copy, 1.0)
            evac(2, blocks(sb_v), ACT.Copy, 1.0)
            log1p(0)
            stick_weights(0)
            log1p(1)
            stick_weights(1)
            log1p(2)
            evac(5, blocks(r_v), ACT.Copy, 1.0)
            stick_weights(2)
            log1p(3)
            stick_weights(3)
            act.wait_ge(ab["rk_turned"], 1)
            for j in range(2):
                op = act.activation(flat(r_kT[:, 2 * j:2 * j + 2, :]), bank[2 + j][:], ACT.Copy)
            op.then_inc(ab["rk"], 1)
            evac(6, blocks(r_gate), ACT.Silu, 1.0)
            for j in range(2):
                act.wait_ge(ab["ret_o"], 2 * j + 2)
                act.activation(flat(r_oT[:, 2 * j:2 * j + 2, :]), bank[4 + j][:], ACT.Copy).then_inc(ab["oT"], 1)

            def experts(l):
                m = moe[l]
                for b in range(NB):
                    act.wait_ge(m["logits_T"], b + 1)
                    act.activation(logits_T[0:ROUTER, b * P:(b + 1) * P], bank[2 * b][0:ROUTER, 0:P],
                                   ACT.Copy).then_inc(m["logits_sb"], 1)
                act.wait_ge(m["group_less"], 1)
                act.activation(g_exp, g_less, ACT.Exp).then_inc(m["group_exp"], 1)
                act.wait_ge(m["second"], 1)
                act.activation(e_ratio, e_max2, ACT.Exp).then_inc(m["second_exp"], 1)

                def silu(i, first=False):
                    act.wait_ge(m["used"], 3 * i + 1)
                    if not first:
                        act.wait_ge(m["hidden"], i)
                    act.activation(e_silu, bank[6][:], ACT.Silu).then_inc(m["silu"], 1)

                def copy_hidden(i):
                    act.wait_ge(m["h_turned"], i + 1)
                    act.activation(flat(e_hT), bank[6][:], ACT.Copy).then_inc(m["hT"], 1)

                def copy_high(i):
                    act.wait_ge(m["used"], 3 * i)
                    act.activation(e_y[:, HALF:D], bank[5][:], ACT.Copy).then_inc(m["y_high"], 1)

                def copy_weights(i):
                    act.wait_ge(m["pickT"], i)
                    act.activation(pick_wT, bank[7][:, 0:S], ACT.Copy).then_inc(m["pickT_sb"], 1)

                silu(0, first=True)
                copy_hidden(0)
                act.wait_ge(m["rounds"], 1)
                n = act.value_load(rounds[0:1, l, 0:1], min_val=PAIRS, max_val=PAIRS * PASSES)
                with act.Fori(1, n) as i:
                    copy_high(i)
                    copy_weights(i)
                    silu(i)
                    copy_hidden(i)
                copy_weights(n)
                copy_high(n)

            mean_squares(1)
            experts(0)

            mean_squares(2)

            def turn_in(done, n, dst, banks, scale, signal):
                act.wait_ge(done, n)
                for j in range(2):
                    op = act.activation(flat(dst[:, 2 * j:2 * j + 2, :]), bank[banks[j]][:], ACT.Copy, scale=scale)
                op.then_inc(signal, 1)

            def prob(t):
                act.wait_ge(cc["masked"], t + 1)
                if t >= 2:
                    act.wait_ge(cc["p_turned"], t - 1)
                for b, cols in enumerate((slice(0, P), slice(P, TRI))):
                    op = act.activation(c_p[:, t % 2, cols], c_s[:, t % 2, cols], ACT.Exp, scale=-1.0,
                                        bias=c_min[:, t, b:b + 1], accum_out=c_sum[:, t, b:b + 1])
                op.then_inc(cc["prob"], 1)
                if t % 4 == 3:
                    act.wait_ge(cc["sink"], t // 4 + 1)
                    act.activation(c_den[:, t - 3:t + 1, :], c_den[:, t - 3:t + 1, :],
                                   ACT.Exp).then_inc(cc["sink_exp"], 1)

            turn_in(cc["k_turned"], 1, c_kT, (6, 7), 1.0, cc["k"])
            turn_in(cc["q_turned"], 1, c_qT[0], (4, 5), -(HD ** -0.5), cc["q"])
            def low(b):
                act.wait_ge(cc["low_turned"], b + 1)
                act.activation(attT[:, 0:4, b * P:(b + 1) * P], bank[1][:].rearrange("p (c n) -> p c n", c=4),
                               ACT.Copy).then_inc(cc["att_low"], 1)

            for t in range(SWA_HEADS):
                if t == 8:
                    turn_in(cc["q_turned"], 2, c_qT[1], (2, 3), -(HD ** -0.5), cc["q"])
                if t == 14:
                    low(0)
                prob(t)
            low(1)
            act.wait_ge(cc["high_turned"], 1)
            act.activation(attT[:, 4:8, 0:P], bank[4][:].rearrange("p (c n) -> p c n", c=4),
                           ACT.Copy).then_inc(cc["att_high_act"], 1)
            mean_squares(3)
            experts(1)
            mean_squares(4)

        @block.tensor
        def _(pe):
            def turn(dst, src):
                return pe.transpose(dst, src, ident)

            def turn_normed(n, b):
                pe.wait_ge(rms_done, NB * n + b + 1)
                for k in range(KD):
                    op = turn(of_block(bank[4 + 2 * b + k // 4], k % 4), hr[:, b, k, :])
                    if k % 4 == 3:
                        op.then_inc(turned, 1)

            def wait_normed(n, b):
                pe.wait_ge(normed, 4 * n + 2 * b + 2)

            def logits_of(l, b):
                wait_normed(2 * l + 1, b)
                if b == 0:
                    pe.wait_ge(late_in, 16)
                for k in range(KD):
                    op = pe.matmul(bank[2 * b][0:ROUTER, 0:P], router[:, l, k, :], hnT[:, k, b * P:(b + 1) * P],
                                   start=(k == 0), stop=(k == KD - 1))
                op.then_inc(moe[l]["logits_T"], 1)

            def turn_logits(l, b):
                pe.wait_ge(moe[l]["logits_sb"], b + 1)
                pe.transpose(bank[1][:, b * CAP:b * CAP + ROUTER], logits_T[0:ROUTER, b * P:(b + 1) * P],
                             ident[0:ROUTER, 0:ROUTER]).then_inc(moe[l]["logits"], 1)

            def project(dst, unit, steps=range(NB * KD)):
                for step in steps:
                    b, k = divmod(step, KD)
                    op = pe.matmul(dst[b][:], hnT[:, k, b * P:(b + 1) * P], unit[:, k, :],
                                   start=(k == 0), stop=(k == KD - 1))
                return op

            pe.wait_ge(early_in, 16)
            for b in range(NB):
                turn_normed(0, b)
            wait_normed(0, 1)

            def in_proj(u):
                s = u % RING
                pe.wait_ge(ab_landed[s], 16 * (u // RING + 1))
                if u in (2, 3, 4):
                    pe.wait_ge(ab["act_evac"], u - 1)
                if u == 5:
                    pe.wait_ge(ab["rope_mul"], 1)
                dst = bank[2 * (u % 2):2 * (u % 2) + 2]
                if u >= 2:
                    op = project(dst, slot_in(s))
                else:
                    for c in range(4):
                        for k in range(KD):
                            op = pe.matmul(dst[c // 2][:, (c % 2) * S:(c % 2 + 1) * S],
                                           slot_in(s)[:, k, c * P:(c + 1) * P], hnT[:, k, :],
                                           start=(k == 0), stop=(k == KD - 1))
                op.then_inc(ab["used"], 1)

            def triangles(dst, kT, qT, pair):
                heads = [(dst[s], head_rows(kT, 2 * pair + s), head_rows(qT, 2 * pair + s)) for s in range(2)]
                for d, k, q in heads:
                    pe.matmul(d[:, 0:S], k[:, 0:P], q, start=True, stop=True, skip_group_check=True)
                for d, k, q in heads:
                    op = pe.matmul(d[:, S:TRI], k[:, P:S], q[:, P:S], start=False, stop=True, skip_group_check=True)
                return op

            def stick_scores(g):
                if g == 0:
                    pe.wait_ge(ab["act_evac"], 2)
                if g >= 2:
                    pe.wait_ge(ab["cat"], g - 1)
                triangles(bank[4 + 2 * (g % 2):6 + 2 * (g % 2)], sb_kT, sb_qT, g).then_inc(ab["z"], 1)

            def stick_sums(g):
                pe.wait_ge(ab["softplus"], 2 * g + 2)
                if g == 0:
                    pe.wait_ge(ones_set, 2)
                for s in range(2):
                    dst, t = bank[4 + 2 * (g % 2) + s], sb_w[:, 2 * (g % 2) + s, :]
                    for cols, src, m in (((0, S), (0, S), neg_from), ((P, S), (S, TRI), neg_ones[:]),
                                         ((S, TRI), (S, TRI), neg_from)):
                        op = pe.matmul(dst[:, cols[0]:cols[1]], m, t[:, src[0]:src[1]], start=False, stop=True,
                                       skip_group_check=True)
                op.then_inc(ab["cum"], 1)

            def stick_values(g):
                pe.wait_ge(ab["weights"], 2 * g + 2)
                if g == 0:
                    pe.wait_ge(ab["act_evac"], 3)
                for b, cols, to in ((0, slice(0, P), 0), (0, slice(P, S), 1), (1, slice(S, TRI), 1)):
                    for s in range(2):
                        head = 2 * g + s
                        op = pe.matmul(bank[4 + 2 * (g % 2) + to][s * HD:(s + 1) * HD, TRI:HALF],
                                       sb_v[:, b, head * HD:(head + 1) * HD], sb_w[:, 2 * (g % 2) + s, cols],
                                       start=(b == 0), stop=(b == to))
                op.then_inc(ab["av"], 1)

            in_proj(0)
            in_proj(1)
            in_proj(2)
            stick_scores(0)
            in_proj(3)
            stick_sums(0)
            stick_scores(1)
            in_proj(4)
            stick_values(0)
            stick_sums(1)
            stick_scores(2)
            in_proj(5)
            stick_values(1)
            stick_sums(2)
            stick_scores(3)
            def turn_r(src):
                for c in range(4):
                    for b in range(NB):
                        lo = (c % 2) * S + b * P
                        op = turn(bank[2 + c // 2][:, lo:lo + P], src[:, b, c * P:(c + 1) * P])
                return op

            pe.wait_ge(ab_landed[0], 32)
            pe.wait_ge(ab["rope_mul"], 2)
            project(bank[0:2], slot_in(0), range(0, 10))
            pe.wait_ge(ab["act_evac"], 4)
            pe.wait_ge(ab["roped"], 2)
            turn_r(r_q).then_inc(ab["rq_turned"], 1)
            stick_values(2)
            stick_sums(3)
            project(bank[0:2], slot_in(0), range(10, 16)).then_inc(ab["used"], 1)
            pe.wait_ge(ab["rq"], 1)
            turn_r(r_k).then_inc(ab["rk_turned"], 1)
            stick_values(3)

            def inner(pair):
                if pair == 0:
                    pe.wait_ge(ab["rk"], 1)
                else:
                    pe.wait_ge(ab["decayed"], 2 * pair)
                triangles(bank[2:4], r_kT, r_qT, pair).then_inc(ab["inner"], 1)

            def ret_values(pair):
                pe.wait_ge(ab["decayed"], 2 * pair + 2)
                if pair == 0:
                    pe.wait_ge(ab["cat"], 3)
                for b, frm, to in ((0, slice(0, S), slice(0, S)), (1, slice(S, TRI), slice(P, S))):
                    for s in range(2):
                        head = 2 * pair + s
                        dst = bank[4 + pair // 2][s * HD:(s + 1) * HD, (pair % 2) * S:(pair % 2 + 1) * S]
                        op = pe.matmul(dst[:, to], r_v[:, b, head * HD:(head + 1) * HD], r_w[:, s, frm],
                                       start=(b == 0), stop=(b == 1), skip_group_check=True)
                op.then_inc(ab["ret_o"], 1)

            def out_proj(t, banks, b, unit, part, steps=range(8)):
                for step in steps:
                    half, c = step // 4, 4 * part + step % 4
                    op = pe.matmul(bank[banks[2 * b + half]][:], t[:, c, b * P:(b + 1) * P],
                                   unit[:, c % 4, half * HALF:(half + 1) * HALF], start=(c == 0), stop=(c == KD - 1))
                return op

            inner(0)
            pe.wait_ge(ab_landed[1], 32)
            pe.wait_ge(ab["act_evac"], 5)
            for pair in range(4):
                if pair < 3:
                    inner(pair + 1)
                ret_values(pair)
                if pair == 0:
                    pe.wait_ge(ab["cat"], 4)
                out_proj(catT, OUT_BANKS, 0, slot_out(1), 0, range(pair, pair + 1))
            pe.wait_ge(ab["oT"], 2)
            for b in range(NB):
                for c in range(4):
                    op = turn(of_block(bank[2 + b], c), r_oT[:, c, b * P:(b + 1) * P])
            op.then_inc(ab["ret_turned"], 1)
            out_proj(catT, OUT_BANKS, 0, slot_out(1), 0, range(4, 8))
            out_proj(catT, OUT_BANKS, 1, slot_out(1), 0).then_inc(ab["used"], 1)
            for b in range(NB):
                pe.wait_ge(ab["gn"], b + 1)
                for c in range(4):
                    op = turn(of_block(bank[2 + b], c), r_c[:, b, c * P:(c + 1) * P])
                op.then_inc(ab["gn_turned"], 1)
            pe.wait_ge(ab_landed[2], 32)
            pe.wait_ge(ab["gn_cat"], 1)
            out_proj(catT, OUT_BANKS, 0, slot_out(2), 1).then_inc(ab["out"], 1)
            pe.wait_ge(ab["gn_cat"], 2)
            out_proj(catT, OUT_BANKS, 1, slot_out(2), 1, range(0, 6))
            turn_normed(1, 0)
            out_proj(catT, OUT_BANKS, 1, slot_out(2), 1, range(6, 8)).then_inc(ab["used"], 1)

            def experts(l):
                m = moe[l]
                logits_of(l, 0)
                turn_normed(2 * l + 1, 1)
                turn_logits(l, 0)
                logits_of(l, 1)
                turn_logits(l, 1)
                pe.wait_ge(m["chosen"], 1)
                one = [chosen[:, b].rearrange("p g e -> p (g e)") for b in range(NB)]
                pe.matmul(bank[0][:, 0:EXPERTS], before, one[0], start=True, stop=True)
                pe.matmul(bank[0][:, EXPERTS:2 * EXPERTS], before, one[1], start=True, stop=False)
                pe.matmul(bank[0][:, EXPERTS:2 * EXPERTS], ones[:], one[0], start=False,
                          stop=True).then_inc(m["ranked"], 1)

                def gather(i):
                    pe.wait_ge(m["pick"], i + 1)
                    for k in range(KD):
                        for b in range(NB):
                            op = pe.matmul(of_block(bank[4 + k // 4], k % 4), hr[:, b, k, :], pick[:, b, :],
                                           start=(b == 0), stop=(b == NB - 1))
                    op.then_inc(m["gathered"], 1)

                def both(i, kind, dst, lhsT, steps, cols, turn_of_gates, odd, second=False):
                    unit = []
                    for j in (2 * kind, 2 * kind + 1):
                        view = as_out if kind == 2 else as_in
                        if kind == 0:
                            pe.wait_ge(m["parked" if odd else "landed"][j], 16 * turn_of_gates)
                            unit.append(view(parked[j] if odd else ring[:, moe_slot(l, j), :]))
                        elif second and j < PARKED:
                            pe.wait_ge(m["parked"][j], 16)
                            unit.append(view(parked[j]))
                        else:
                            skipped = j < PARKED and not (isinstance(i, int) and i == 0)
                            pe.wait_ge(m["landed"][j], 16 * i if skipped else 16 * (i + 1))
                            unit.append(view(ring[:, moe_slot(l, j), :]))
                    for q in range(steps):
                        for s in range(2):
                            rows = slice(s * CAP, (s + 1) * CAP)
                            op = pe.matmul(dst[rows, :], lhsT[:, q, rows], unit[s][:, q, cols],
                                           start=(q == 0), stop=(q == steps - 1))
                    return op

                def turn_weights(i):
                    pe.wait_ge(m["pick_w"], i)
                    pe.wait_ge(m["hidden"], i)
                    for b in range(NB):
                        op = turn(of_block(bank[7], b), pick_w[:, b, :])
                    op.then_inc(m["pickT"], 1)

                def combine(i, first=False, last=False):
                    pe.wait_ge(m["y_low"], i)
                    pe.wait_ge(m["y_high"], i)
                    pe.wait_ge(m["pickT_sb"], i)
                    for half in range(2):
                        for b in range(NB):
                            op = pe.matmul(bank[2 * b + half][:], pick_wT[:, b * P:(b + 1) * P],
                                           e_y[:, half * HALF:(half + 1) * HALF], start=first, stop=last,
                                           skip_group_check=True)
                            if last and half:
                                op.then_inc(m["combined"], 1)

                def pair(i, turn_of_gates, odd, first=False, second=False, final=False):
                    if not first:
                        turn_weights(i)
                    pe.wait_ge(m["xe"], i + 1)
                    if not first:
                        pe.wait_ge(m["hT"], i)
                    both(i, 0, bank[6], xeT, KD, slice(0, DE), turn_of_gates, odd, second).then_inc(m["used"], 1)
                    if not first:
                        pe.wait_ge(m["pickT_sb"], i)
                    both(i, 1, bank[7], xeT, KD, slice(0, DE), turn_of_gates, odd, second).then_inc(m["used"], 1)
                    if not first:
                        pe.wait_ge(m["y_low"], i)
                        pe.wait_ge(m["y_high"], i)
                    if not final:
                        gather(i + 1)
                    pe.wait_ge(m["hidden"], i + 1)
                    for mh in range(MH):
                        op = turn(of_block(bank[6], mh), e_h[:, mh * P:(mh + 1) * P])
                    op.then_inc(m["h_turned"], 1)
                    if not first:
                        combine(i, first=second)
                    if final:
                        turn_weights(n)
                    pe.wait_ge(m["hT"], i + 1)
                    if not final:
                        pe.wait_ge(m["xe"], i + 2)
                    both(i, 2, bank[4], e_hT, MH, slice(0, HALF), turn_of_gates, odd, second).then_inc(m["down_low"], 1)
                    both(i, 2, bank[5], e_hT, MH, slice(HALF, D), turn_of_gates, odd, second).then_inc(m["used"], 1)

                gather(0)
                pe.wait_ge(m["fullest"], 1)
                pe.transpose(bank[2][0:1, 0:P], fullest, ident).then_inc(m["fullest_row"], 1)
                pair(0, 1, False, first=True)
                pair(1, 1, True, second=True)
                pe.wait_ge(m["rounds"], 1)
                n = pe.value_load(rounds[0:1, l, 0:1], min_val=PAIRS, max_val=PAIRS * PASSES)
                last = pe.value_load(rounds[0:1, l, 1:2], min_val=PAIRS - 1, max_val=PAIRS * PASSES - 1)
                half = pe.value_load(rounds[0:1, l, 3:4], min_val=PAIRS // 2 - 1, max_val=PAIRS * PASSES // 2 - 1)
                pair(2, 2, False)
                with pe.Fori(1, half) as t:
                    pair(2 * t + 1, t + 1, True)
                    pair(2 * t + 2, t + 2, False)
                pair(last, half + 1, True, final=True)
                combine(n, last=True)

            experts(0)

            pe.wait_ge(c_landed[0], 16)
            for b in range(NB):
                turn_normed(2, b)
                wait_normed(2, b)
                op = project(bank[0:2], slot_in(c_slot(0)), range(b * KD, (b + 1) * KD))
            op.then_inc(cc["used"], 1)
            pe.wait_ge(c_landed[1], 16)
            project(bank[2:4], slot_in(c_slot(1)), range(0, 12))
            pe.wait_ge(cc["roped"], 1)
            for c in range(4):
                for b in range(NB):
                    op = turn(bank[6 + c // 2][:, (c % 2) * S + b * P:(c % 2) * S + (b + 1) * P],
                              c_k[:, b, c * P:(c + 1) * P])
            op.then_inc(cc["k_turned"], 1)
            project(bank[2:4], slot_in(c_slot(1)), range(12, 16)).then_inc(cc["used"], 1)

            def turn_q(j, banks):
                pe.wait_ge(cc["roped"], j + 2)
                for c in range(4):
                    for b in range(NB):
                        lo = (c % 2) * S + b * P
                        op = turn(bank[banks[c // 2]][:, lo:lo + P],
                                  c_q[:, b, j * HALF + c * P:j * HALF + (c + 1) * P])
                op.then_inc(cc["q_turned"], 1)

            def high_q(lo, hi):
                return project(bank[0:2], slot_in(c_slot(2)), range(lo, hi))

            def swa_scores(pair):
                if pair == 0:
                    pe.wait_ge(cc["k"], 1)
                    pe.wait_ge(cc["q"], 1)
                else:
                    pe.wait_ge(cc["masked"], 2 * pair)
                if pair == SWA_HEADS // 4:
                    pe.wait_ge(cc["q"], 2)
                heads = [(bank[4 + s], head_rows(c_qT[pair // 4], s, pair % 4), head_rows(c_kT, s, pair // 2)) for s in range(2)]
                for dst, qT, kT in heads:
                    pe.matmul(dst[:, 0:P], qT[:, 0:P], kT[:, 0:P], start=True, stop=True)
                for dst, qT, kT in heads:
                    pe.matmul(dst[:, P:TRI], qT[:, P:S], kT, start=True, stop=True).then_inc(cc["scores"], 1)

            def turn_p(pair):
                for t in (2 * pair, 2 * pair + 1):
                    pe.wait_ge(cc["prob"], t + 1)
                    if t >= 2:
                        pe.wait_ge(cc["pT"], t - 1)
                    for j in range(3):
                        op = turn(of_block(bank[6 + t % 2], j), c_p[:, t % 2, j * P:(j + 1) * P])
                    op.then_inc(cc["p_turned"], 1)

            def swa_values(pair):
                g = pair // 2
                if pair == 0:
                    pe.wait_ge(cc["biased"], 3)
                if pair == 4:
                    pe.wait_ge(cc["o_norm"], 1)
                if pair == 6:
                    pe.wait_ge(cc["att_low"], 2)
                for t in (2 * pair, 2 * pair + 1):
                    pe.wait_ge(cc["pT"], t + 1)
                    pT, dst, cols = c_pT[:, t % 2, :], bank[g % 2], slice(g * HD, (g + 1) * HD)
                    lo, hi = (dst[:, b * S + (t % 4) * HD:b * S + (t % 4 + 1) * HD] for b in range(NB))
                    pe.matmul(lo, pT[:, 0:P], c_v[:, 0, cols], start=True, stop=True)
                    pe.matmul(hi, pT[:, P:S], c_v[:, 0, cols], start=True, stop=False)
                    pe.matmul(hi, pT[:, S:TRI], c_v[:, 1, cols], start=False, stop=True).then_inc(cc["o"], 1)

            def turn_low(b):
                if b == 0:
                    pe.wait_ge(cc["o_norm"], 2)
                else:
                    pe.wait_ge(cc["att_low"], 1)
                for c in range(4):
                    op = turn(of_block(bank[1], c), c_o[:, b, c * P:(c + 1) * P])
                op.then_inc(cc["low_turned"], 1)

            def out_low(lo, hi):
                return out_proj(attT, C_OUT_BANKS, 0, slot_out(c_slot(3)), 0, range(lo, hi))

            pe.wait_ge(c_landed[2], 16)
            pe.wait_ge(cc["biased"], 1)
            high_q(0, 7)
            turn_q(0, (4, 5))
            high_q(7, 9)
            swa_scores(0)
            high_q(9, 12)
            swa_scores(1)
            turn_p(0)
            high_q(12, 16).then_inc(cc["used"], 1)
            swa_scores(2)
            turn_p(1)
            swa_values(0)
            swa_scores(3)
            turn_p(2)
            swa_values(1)
            turn_q(1, (2, 3))
            swa_scores(4)
            turn_p(3)
            swa_values(2)
            swa_scores(5)
            turn_p(4)
            swa_values(3)
            swa_scores(6)
            turn_p(5)
            swa_values(4)
            swa_scores(7)
            turn_p(6)
            turn_low(0)
            swa_values(5)
            pe.wait_ge(c_landed[3], 16)
            pe.wait_ge(cc["att_low"], 1)
            out_low(0, 2)
            turn_low(1)
            turn_p(7)
            out_low(2, 5)
            swa_values(6)
            out_low(5, 8)
            swa_values(7)
            out_proj(attT, C_OUT_BANKS, 1, slot_out(c_slot(3)), 0).then_inc(cc["used"], 1)
            pe.wait_ge(cc["o_norm"], 4)
            for b in range(NB):
                for c in range(4):
                    op = turn(of_block(bank[4 + b], c), c_o[:, b, (4 + c) * P:(5 + c) * P])
                op.then_inc(cc["high_turned"], 1)
            pe.wait_ge(c_landed[4], 16)
            pe.wait_ge(cc["att_high_act"], 1)
            out_proj(attT, C_OUT_BANKS, 0, slot_out(c_slot(4)), 1).then_inc(cc["out"], 1)
            pe.wait_ge(cc["att_high_dve"], 1)
            out_proj(attT, C_OUT_BANKS, 1, slot_out(c_slot(4)), 1, range(0, 6))
            turn_normed(3, 0)
            out_proj(attT, C_OUT_BANKS, 1, slot_out(c_slot(4)), 1, range(6, 8)).then_inc(cc["used"], 1)
            experts(1)

        @block.vector
        def _(dve):
            steps = [0]

            def link(op):
                steps[0] += 1
                op.then_inc(dve_step, 1)
                dve.wait_ge(dve_step, steps[0])

            def norm(n, b):
                dve.wait_ge(rooted, NB * n + b + 1)
                if n < 2 * DEPTH:
                    dve.tensor_scalar(hr[:, b].rearrange("p k c -> p c k"),
                                      h[:, b, :].rearrange("p (c k) -> p c k", k=KD), rstd[:, n, b:b + 1], None,
                                      ALU.mult).then_inc(rms_done, 1)
                else:
                    dve.scalar_tensor_tensor(out=flat(hr[:, b]), in0=h[:, b, :], scalar=rstd[:, n, b:b + 1],
                                             in1=final_gain, op0=ALU.mult, op1=ALU.mult).then_inc(out_ready, 1)

            def spread_normed(n, b):
                for q in range(2):
                    dve.wait_ge(turned, 4 * n + 2 * b + q + 1)
                    dve.tensor_tensor(hnT[:, 4 * q:4 * q + 4, b * P:(b + 1) * P],
                                      bank[4 + 2 * b + q][:].rearrange("p (k c) -> p k c", k=4),
                                      spread(gains[:, n, 4 * q:4 * q + 4], P), ALU.mult).then_inc(normed, 1)

            dve.wait_ge(early_in, 16)
            for b in range(NB):
                norm(0, b)
            for b in range(NB):
                spread_normed(0, b)

            def softplus(g):
                for s in range(2):
                    t = sb_w[:, 2 * (g % 2) + s, :]
                    dve.wait_ge(ab["log1p"], 2 * g + s + 1)
                    link(dve.scalar_tensor_tensor(out=t, in0=bank[4 + 2 * (g % 2) + s][:, 0:TRI], scalar=0.0, in1=t,
                                                  op0=ALU.max, op1=ALU.add))
                    dve.tensor_tensor(diagonal(t), diagonal(t), before2, ALU.mult).then_inc(ab["softplus"], 1)

            def causal_weights(g):
                for s in range(2):
                    t = sb_w[:, 2 * (g % 2) + s, :]
                    dve.wait_ge(ab["expw"], 2 * g + s + 1)
                    dve.scalar_tensor_tensor(out=diagonal(t), in0=diagonal(t), scalar=3e38, in1=before2, op0=ALU.min,
                                             op1=ALU.mult).then_inc(ab["weights"], 1)

            def concat(g):
                dve.wait_ge(ab["av"], g + 1)
                for b in range(NB):
                    op = dve.tensor_copy(catT[:, g, b * P:(b + 1) * P], bank[4 + 2 * (g % 2) + b][:, TRI:HALF])
                op.then_inc(ab["cat"], 1)

            def rotate(v):
                dve.wait_ge(ab["used"], 4 + v)
                if v:
                    dve.wait_ge(ab["roped"], v)
                for b in range(NB):
                    src = bank[2 * ((3 + v) % 2) + b][:]
                    dve.tensor_tensor(per_head(rope_a[:, b, :], 8), per_head(src, 8), over_heads(cos[:, b, :], 8), ALU.mult)
                    op = dve.tensor_tensor(per_head(rope_b[:, b, :], 8), swapped(src, 8), over_heads(sin[:, b, :], 8),
                                           ALU.mult)
                op.then_inc(ab["rope_mul"], 1)

            softplus(0)
            rotate(0)
            causal_weights(0)
            softplus(1)
            rotate(1)
            concat(0)
            causal_weights(1)
            softplus(2)
            concat(1)
            causal_weights(2)
            softplus(3)
            concat(2)
            causal_weights(3)
            dve.wait_ge(ab["rq_turned"], 1)
            for j in range(2):
                op = dve.tensor_copy(flat(r_qT[:, 2 * j:2 * j + 2, :]), bank[2 + j][:])
            op.then_inc(ab["rq"], 1)
            concat(3)
            dve.wait_ge(decay_in, 16)
            for head in range(RET_HEADS):
                dve.wait_ge(ab["inner"], head // 2 + 1)
                if head >= 2:
                    dve.wait_ge(ab["ret_o"], head // 2)
                dve.tensor_tensor(r_w[:, head % 2, :], bank[2 + head % 2][:, 0:TRI], decay[:, head, :],
                                  ALU.mult).then_inc(ab["decayed"], 1)
            dve.wait_ge(ab["ret_turned"], 1)
            by_head = [bank[2 + b][:].rearrange("p (h e) -> p h e", e=HD) for b in range(NB)]
            heads_of = [t.rearrange("p b (h e) -> p (b h) e", e=HD) for t in (r_c, r_sq)]
            sums = gn_sum.rearrange("p b h -> p (b h)")
            dve.tensor_reduce(gn_sum[:, 0], by_head[0], AX_X, ALU.add)
            link(dve.tensor_reduce(gn_sum[:, 1], by_head[1], AX_X, ALU.add))
            for b in range(NB):
                op = dve.scalar_tensor_tensor(out=r_c[:, b].rearrange("p (h e) -> p h e", e=HD), in0=spread(gn_sum[:, b], HD),
                                              scalar=-1.0 / HD, in1=by_head[b], op0=ALU.mult, op1=ALU.add)
            link(op)
            link(dve.tensor_tensor(flat(r_sq), flat(r_c), flat(r_c), ALU.mult))
            dve.tensor_reduce(sums, heads_of[1], AX_X, ALU.add).then_inc(ab["gn_var"], 1)
            dve.wait_ge(ab["act_evac"], 5)
            link(dve.tensor_tensor(flat(r_c), flat(r_c), flat(r_gate), ALU.mult))
            dve.wait_ge(ab["gn_root"], 1)
            for b in range(NB):
                rows = heads_of[0][:, b * RET_HEADS:(b + 1) * RET_HEADS, :]
                dve.scalar_tensor_tensor(out=rows, in0=rows, scalar=HD ** 0.5, in1=spread(gn_rstd[:, b], HD),
                                         op0=ALU.mult, op1=ALU.mult).then_inc(ab["gn"], 1)
            for b in range(NB):
                dve.wait_ge(ab["gn_turned"], b + 1)
                dve.tensor_tensor(catT[:, 4:8, b * P:(b + 1) * P], bank[2 + b][:].rearrange("p (c n) -> p c n", c=4),
                                  spread(gn_gain, P), ALU.mult).then_inc(ab["gn_cat"], 1)

            def residual(b, banks):
                for half in range(2):
                    cols = slice(half * HALF, (half + 1) * HALF)
                    op = dve.tensor_tensor(h[:, b, cols], h[:, b, cols], bank[banks[2 * b + half]][:], ALU.add)
                op.then_inc(h_done, 1)

            dve.wait_ge(ab["out"], 1)
            residual(0, OUT_BANKS)
            norm(1, 0)
            spread_normed(1, 0)
            dve.wait_ge(ab["used"], AB_UNITS)
            residual(1, OUT_BANKS)
            norm(1, 1)
            spread_normed(1, 1)

            def experts(l):
                m = moe[l]
                dve.wait_ge(m["logits"], 2)
                rows = bank[1][:, 0:NB * CAP].rearrange("p (b n) -> p b n", b=NB)
                g_log = rows[:, :, 0:GROUPS]
                e_log = rows[:, :, GROUPS:ROUTER].rearrange("p b (g e) -> p b g e", g=GROUPS)
                firsts = first8.unsqueeze(1).broadcast_to([P, NB * GROUPS, PER_GROUP])

                def by_group(t):
                    return t.rearrange("p b g e -> p (b g) e")

                dve.tensor_reduce(g_max, g_log, AX_X, ALU.max)
                link(dve.tensor_reduce(e_max, e_log, AX_X, ALU.max))
                dve.tensor_tensor(g_less, g_log, spread(g_max, GROUPS), ALU.subtract).then_inc(m["group_less"], 1)
                link(dve.tensor_tensor(e_less, e_log, spread(e_max, PER_GROUP), ALU.subtract))
                dve.wait_ge(m["group_less"], 1)
                dve.scalar_tensor_tensor(out=g_score, in0=g_less, scalar=0.0,
                                         in1=first4.unsqueeze(1).broadcast_to([P, NB, GROUPS]),
                                         op0=ALU.is_ge, op1=ALU.mult)
                link(dve.scalar_tensor_tensor(out=by_group(e_score), in0=by_group(e_less), scalar=0.0, in1=firsts, op0=ALU.is_ge, op1=ALU.mult))
                dve.tensor_reduce(g_best, g_score, AX_X, ALU.max)
                link(dve.tensor_reduce(e_best, e_score, AX_X, ALU.max))
                dve.tensor_tensor(g_hot, g_score, spread(g_best, GROUPS), ALU.is_equal)
                link(dve.tensor_tensor(e_hot1, e_score, spread(e_best, PER_GROUP), ALU.is_equal))
                link(dve.scalar_tensor_tensor(out=by_group(e_rest), in0=by_group(e_hot1), scalar=-BIG, in1=by_group(e_less), op0=ALU.mult, op1=ALU.add))
                dve.tensor_reduce(e_max2, e_rest, AX_X, ALU.max).then_inc(m["second"], 1)
                dve.wait_ge(m["second"], 1)
                link(dve.tensor_tensor(e_less, e_rest, spread(e_max2, PER_GROUP), ALU.subtract))
                link(dve.scalar_tensor_tensor(out=by_group(e_score), in0=by_group(e_less), scalar=0.0, in1=firsts, op0=ALU.is_ge, op1=ALU.mult))
                link(dve.tensor_reduce(e_best, e_score, AX_X, ALU.max))
                link(dve.tensor_tensor(e_hot2, e_score, spread(e_best, PER_GROUP), ALU.is_equal))
                link(dve.tensor_tensor(e_both, e_hot1, e_hot2, ALU.add))
                dve.tensor_tensor(chosen, e_both, spread(g_hot, PER_GROUP), ALU.mult).then_inc(m["chosen"], 1)

                dve.wait_ge(m["ranked"], 1)
                ranks = rank.rearrange("p b g e -> p b (g e)")

                def rank_of_pass(j):
                    return dve.tensor_scalar(rank_all[:, :, j * EXPERTS:(j + 1) * EXPERTS], ranks, -1.0 - CAP * j,
                                             None, ALU.add)

                link(dve.scalar_tensor_tensor(out=rank.rearrange("p b g e -> p (b g e)"), in0=bank[0][:, 0:NB * EXPERTS],
                                              scalar=1.0, in1=chosen.rearrange("p b g e -> p (b g e)"),
                                              op0=ALU.add, op1=ALU.mult))
                link(rank_of_pass(0))

                def one_hot(i, first=False):
                    if not first:
                        dve.wait_ge(m["pick_w"], i)
                    dve.tensor_tensor(pair_rows(pick), slots.unsqueeze(1).unsqueeze(1).broadcast_to([P, NB, 2, CAP]),
                                      of_pair(rank_all, i), ALU.is_equal).then_inc(m["pick"], 1)

                one_hot(0, first=True)
                dve.tensor_reduce(fullest, rank.rearrange("p b g e -> p (b g e)"), AX_X, ALU.max).then_inc(m["fullest"], 1)
                for j in range(1, PASSES):
                    op = rank_of_pass(j)
                link(op)

                dve.wait_ge(m["group_exp"], 1)
                link(dve.tensor_reduce(g_sum, g_exp, AX_X, ALU.add))
                dve.wait_ge(m["second_exp"], 1)
                link(dve.tensor_scalar(e_den, e_ratio, 1.0, None, ALU.add))
                link(dve.tensor_tensor(e_den, e_den, spread(g_sum, GROUPS), ALU.mult))
                link(dve.reciprocal(gate1, e_den))
                link(dve.tensor_tensor(gate1, gate1, g_hot, ALU.mult))
                link(dve.tensor_tensor(gate2, gate1, e_ratio, ALU.mult))
                dve.tensor_tensor(e_gate1, e_hot1, spread(gate1, PER_GROUP), ALU.mult)
                link(dve.tensor_tensor(e_gate2, e_hot2, spread(gate2, PER_GROUP), ALU.mult))
                for j in range(PASSES):
                    op = dve.tensor_tensor(gate_all[:, :, j * EXPERTS:(j + 1) * EXPERTS], e_gate1.rearrange("p b g e -> p b (g e)"),
                                           e_gate2.rearrange("p b g e -> p b (g e)"), ALU.add)
                op.then_inc(m["gates"], 1)

                def take_rows(i):
                    dve.wait_ge(m["gathered"], i + 1)
                    for q in range(2):
                        op = dve.tensor_tensor(xeT[:, 4 * q:4 * q + 4, :], bank[4 + q][:].rearrange("p (k c) -> p k c", k=4),
                                               spread(gains[:, 2 * l + 1, 4 * q:4 * q + 4], P), ALU.mult)
                    op.then_inc(m["xe"], 1)

                def hidden(i):
                    dve.wait_ge(m["silu"], i + 1)
                    dve.wait_ge(m["used"], 3 * i + 2)
                    dve.tensor_tensor(e_h, e_silu, bank[7][:], ALU.mult).then_inc(m["hidden"], 1)

                def copy_low(i):
                    dve.wait_ge(m["down_low"], i)
                    dve.tensor_copy(e_y[:, 0:HALF], bank[4][:]).then_inc(m["y_low"], 1)

                take_rows(0)
                dve.wait_ge(m["fullest_row"], 1)
                link(dve.tensor_reduce(fullest_all[0:1], bank[2][0:1, 0:P], AX_X, ALU.max))
                for j in range(1, PASSES):
                    op = dve.tensor_scalar(more[0:1, j - 1:j], fullest_all[0:1], CAP * j + 0.5, float(PAIRS),
                                           ALU.is_ge, ALU.mult)
                link(op)
                link(dve.tensor_reduce(fullest_all[0:1], more[0:1], AX_X, ALU.add))
                dve.tensor_scalar(rounds[0:1, l, 0:1], fullest_all[0:1], float(PAIRS), None, ALU.add)
                dve.tensor_scalar(rounds[0:1, l, 1:2], fullest_all[0:1], float(PAIRS - 1), None, ALU.add)
                dve.tensor_scalar(rounds[0:1, l, 2:3], fullest_all[0:1], float(PAIRS - 2), None, ALU.add)
                dve.tensor_scalar(rounds[0:1, l, 3:4], fullest_all[0:1], 0.5, float(PAIRS // 2 - 1),
                                  ALU.mult, ALU.add).then_inc(m["rounds"], 1)
                one_hot(1)
                hidden(0)
                take_rows(1)
                dve.wait_ge(m["rounds"], 1)
                n = dve.value_load(rounds[0:1, l, 0:1], min_val=PAIRS, max_val=PAIRS * PASSES)
                last = dve.value_load(rounds[0:1, l, 1:2], min_val=PAIRS - 1, max_val=PAIRS * PASSES - 1)
                with dve.Fori(1, last) as i:
                    copy_low(i)
                    one_hot(i + 1)
                    hidden(i)
                    take_rows(i + 1)
                copy_low(last)
                hidden(last)
                copy_low(n)
                for b in range(NB):
                    dve.wait_ge(m["combined"], b + 1)
                    residual(b, [0, 1, 2, 3])

            dve.wait_ge(late_in, 16)
            experts(0)

            for b in range(NB):
                norm(2, b)
                spread_normed(2, b)
            dve.wait_ge(rows_in[0], 48)
            link(dve.tensor_scalar(sink_neg[:], sinks_b[:], -1.0, None, ALU.mult))

            def add_bias(u):
                heads = SB_HEADS if u else KV_HEADS
                w = heads * HD
                dve.wait_ge(cc["used"], u + 1)
                for b in range(NB):
                    op = dve.tensor_tensor(c_in[:, b, :], bank[2 * (u % 2) + b][:], c_bin[:, C_COLS[u]:C_COLS[u] + HALF],
                                           ALU.add)
                op.then_inc(cc["biased"], 1)
                dve.wait_ge(cc["biased"], u + 1)
                if u == 0:
                    dve.tensor_copy(c_v, c_in[:, :, w:2 * w])
                for b in range(NB):
                    op = dve.tensor_tensor(per_head(c_a[:, b, 0:w], heads), per_head(c_in[:, b, 0:w], heads),
                                           over_heads(cos[:, b, :], heads), ALU.mult)
                link(op)

            def add_swapped(u):
                w = (SB_HEADS if u else KV_HEADS) * HD
                dve.wait_ge(cc["rope_swap"], u + 1)
                if u:
                    op = dve.tensor_tensor(c_q[:, :, (u - 1) * HALF:u * HALF], c_a, c_b, ALU.add)
                else:
                    for copy in range(2):
                        for b in range(NB):
                            op = dve.tensor_tensor(
                                c_k[:, b].rearrange("p (h a c) -> p h a c", h=KV_HEADS, a=2)[:, :, copy, :],
                                c_a[:, b, 0:w].rearrange("p (h c) -> p h c", c=HD),
                                c_b[:, b, 0:w].rearrange("p (h c) -> p h c", c=HD), ALU.add)
                op.then_inc(cc["roped"], 1)

            for u in range(2):
                add_bias(u)
                add_swapped(u)

            def masked(t):
                dve.wait_ge(cc["scores"], t + 1)
                if t >= 2:
                    dve.wait_ge(cc["prob"], t - 1)
                for b, cols in enumerate((slice(0, P), slice(P, TRI))):
                    op = dve.tensor_tensor_reduce(out=c_s[:, t % 2, cols], in0=bank[4 + t % 2][:, cols],
                                                  in1=swa_mask[:, cols], scale=1.0, scalar=sink_neg[:, t:t + 1],
                                                  op0=ALU.add, op1=ALU.min, accum_out=c_min[:, t, b:b + 1])
                op.then_inc(cc["masked"], 1)
                if t % 4 == 3:
                    dve.wait_ge(cc["masked"], t + 1)
                    dve.tensor_tensor(c_den[:, t - 3:t + 1, :], c_min[:, t - 3:t + 1, :],
                                      spread(sink_neg[:, t - 3:t + 1], NB), ALU.subtract).then_inc(cc["sink"], 1)

            def copy_p(t):
                dve.wait_ge(cc["p_turned"], t + 1)
                if t >= 2:
                    dve.wait_ge(cc["o"], t - 1)
                dve.tensor_copy(c_pT[:, t % 2, :], bank[6 + t % 2][:, 0:TRI]).then_inc(cc["pT"], 1)

            def normalise(g):
                hs = slice(4 * g, 4 * g + 4)
                dve.wait_ge(cc["prob"], 4 * g + 4)
                dve.wait_ge(cc["sink_exp"], g + 1)
                link(dve.tensor_tensor(c_den[:, hs, :], c_den[:, hs, :], c_sum[:, hs, :], ALU.add))
                link(dve.reciprocal(c_den[:, hs, :], c_den[:, hs, :]))
                dve.wait_ge(cc["o"], 4 * g + 4)
                for b in range(NB):
                    op = dve.tensor_tensor(c_o[:, b, g * S:(g + 1) * S].rearrange("p (h e) -> p h e", e=HD),
                                           bank[g % 2][:, b * S:(b + 1) * S].rearrange("p (h e) -> p h e", e=HD),
                                           spread(c_den[:, hs, b], HD), ALU.mult)
                op.then_inc(cc["o_norm"], 1)

            for pair in range(SWA_HEADS // 2 + 1):
                if pair < SWA_HEADS // 2:
                    masked(2 * pair)
                    masked(2 * pair + 1)
                if pair > 0:
                    copy_p(2 * pair - 2)
                    copy_p(2 * pair - 1)
                if pair == 1:
                    add_bias(2)
                if pair == 2:
                    add_swapped(2)
                if pair >= 4 and pair % 2 == 0:
                    normalise(pair // 2 - 2)
            normalise(3)
            dve.wait_ge(cc["high_turned"], 2)
            dve.tensor_copy(attT[:, 4:8, P:S], bank[5][:].rearrange("p (c n) -> p c n", c=4)).then_inc(cc["att_high_dve"], 1)
            dve.wait_ge(cc["bias_h"], 1)
            dve.wait_ge(cc["out"], 1)
            residual(0, C_OUT_BANKS)
            norm(3, 0)
            spread_normed(3, 0)
            dve.wait_ge(cc["used"], C_UNITS)
            residual(1, C_OUT_BANKS)
            norm(3, 1)
            spread_normed(3, 1)
            experts(1)
            dve.wait_ge(rows_in[1], 16)
            for b in range(NB):
                norm(4, b)


_INS = ["x", "w_in_ab", "w_out_ab", "w_in_c", "b_in_c", "sinks", "w_out_c", "b_out_c", "w_gate", "w_up",
        "w_down", "final_norm_g"]
_TABLED = ["attn_norm_g", "ffn_norm_g", "ret_gn_g", "w_group", "w_expert_router"]


def kernel(**inputs):
    import concourse.bacc as bacc
    from concourse.bass_utils import run_bass_kernel_spmd

    nc = bacc.Bacc("TRN2", target_bir_lowering=False, num_devices=1)
    arrays = {f"in_{name}": np.ascontiguousarray(inputs[name]) for name in _INS}
    arrays["early_table"], arrays["late_table"], arrays["decay_table"] = tables(
        *(np.asarray(inputs[name]) for name in _TABLED))
    args = [nc.dram_tensor(name, a.shape, F32, kind="ExternalInput").ap() for name, a in arrays.items()]
    args.append(nc.dram_tensor("out", (1, S, D), F32, kind="ExternalOutput").ap())
    hybrid_trunk(nc, *args)
    return run_bass_kernel_spmd(nc, [arrays], core_ids=[0]).results[0]["out"]
```
